# Optimizing a Trainium2 kernel written in Bass

```python
import math
import jax, jax.numpy as jnp
from jax import lax
import numpy as np
import jax
import jax.numpy as jnp

D_MODEL = 1024
BATCH = 1
SEQ = 256
DEPTH = 1

N_MEM = 256
EPS = 1e-6
GLA_HEADS = 4
GLA_DK = D_MODEL // (2 * GLA_HEADS)
GLA_DV = D_MODEL // GLA_HEADS
GLA_RANK = 16
GLA_GATE_NORM = 16.0
GLA_CHUNK = 64
DSA_HEADS = 8
DSA_KV_HEADS = 2
DSA_HD = D_MODEL // DSA_HEADS
IDX_HEADS = 8
IDX_DIM = 64
TOPK_MAX = 256
Q_BLOCK = 128
REL_BUCKETS = 32
REL_MAX_DIST = 128
X_HEADS = 4
X_HD = D_MODEL // X_HEADS
N_BRANCH = 3

SPLIT_SIZES = (
    GLA_HEADS * GLA_DK,
    GLA_HEADS * GLA_DK,
    GLA_HEADS * GLA_DV,
    GLA_RANK,
    GLA_HEADS * GLA_DV,
    DSA_HEADS * DSA_HD,
    DSA_KV_HEADS * DSA_HD,
    DSA_KV_HEADS * DSA_HD,
    IDX_HEADS * IDX_DIM,
    IDX_DIM,
    IDX_HEADS,
    DSA_HEADS * DSA_HD,
    X_HEADS * X_HD,
    X_HEADS * X_HD,
    N_BRANCH * D_MODEL,
)
W_IN_COLS = 11352


def rmsnorm(x, g):
    xf = x.astype(jnp.float32)
    y = xf * lax.rsqrt(jnp.mean(xf * xf, axis=-1, keepdims=True) + EPS)
    return (y * g.astype(jnp.float32)).astype(x.dtype)

def split_cols(u):
    offsets = np.cumsum(np.array(SPLIT_SIZES))[:-1].tolist()
    return jnp.split(u, offsets, axis=-1)

def t5_bucket(dist):
    max_exact = REL_BUCKETS // 2
    d = jnp.maximum(dist, 1).astype(jnp.float32)
    large = max_exact + (jnp.log(d / max_exact) / math.log(REL_MAX_DIST / max_exact)
                         * (REL_BUCKETS - max_exact)).astype(jnp.int32)
    large = jnp.minimum(large, REL_BUCKETS - 1)
    return jnp.where(dist < max_exact, dist, large)

def gla_mixer(q, k, v, a_low, z, w_a_up, b_a, g_head):
    B, L, _ = q.shape
    H, dk, dv, C = GLA_HEADS, GLA_DK, GLA_DV, GLA_CHUNK
    nc = L // C
    q = q.reshape(B, nc, C, H, dk) * (dk ** -0.5)
    k = k.reshape(B, nc, C, H, dk)
    v = v.reshape(B, nc, C, H, dv)
    log_a = jax.nn.log_sigmoid((a_low @ w_a_up + b_a).astype(jnp.float32)) / GLA_GATE_NORM
    b = jnp.cumsum(log_a.reshape(B, nc, C, H, dk), axis=2)
    b_last = b[:, :, -1:]
    q_d = q * jnp.exp(b).astype(q.dtype)
    k_d = k * jnp.exp(-b).astype(k.dtype)
    k_t = k * jnp.exp(b_last - b).astype(k.dtype)
    decay = jnp.exp(b_last[:, :, 0]).astype(q.dtype)
    causal = jnp.tril(jnp.ones((C, C), dtype=bool))
    att = jnp.einsum('bnthd,bnshd->bnhts', q_d, k_d)
    att = jnp.where(causal, att, jnp.zeros_like(att))
    o_intra = jnp.einsum('bnhts,bnshv->bnthv', att, v)

    def step(state, inp):
        qc, kc, vc, dc = inp
        o = jnp.einsum('bthd,bhdv->bthv', qc, state)
        state = dc[..., None] * state + jnp.einsum('bthd,bthv->bhdv', kc, vc)
        return state, o

    s0 = jnp.zeros((B, H, dk, dv), q.dtype)
    xs = (q_d.transpose(1, 0, 2, 3, 4), k_t.transpose(1, 0, 2, 3, 4),
          v.transpose(1, 0, 2, 3, 4), decay.transpose(1, 0, 2, 3))
    _, o_inter = lax.scan(step, s0, xs)
    o = o_intra + o_inter.transpose(1, 0, 2, 3, 4)
    o = rmsnorm(o.reshape(B, L, H, dv), g_head)
    return o.reshape(B, L, H * dv) * jax.nn.silu(z)

def dsa_mixer(q, k, v, iq, ik, iw, z, rel_bias):
    B, L, _ = q.shape
    topk = min(TOPK_MAX, L // 4)
    nb = L // Q_BLOCK
    KV = DSA_KV_HEADS
    G = DSA_HEADS // KV
    q = q.reshape(B, nb, Q_BLOCK, KV, G, DSA_HD) * (DSA_HD ** -0.5)
    k = k.reshape(B, L, KV, DSA_HD)
    v = v.reshape(B, L, KV, DSA_HD)
    iq = iq.reshape(B, nb, Q_BLOCK, IDX_HEADS, IDX_DIM)
    iw = iw.reshape(B, nb, Q_BLOCK, IDX_HEADS) * (IDX_HEADS ** -0.5) * (IDX_DIM ** -0.5)
    ik_f = ik.astype(jnp.float32)
    key_pos = jnp.arange(L, dtype=jnp.int32)

    def block(inp):
        qb, iqb, iwb, start = inp
        q_pos = start + jnp.arange(Q_BLOCK, dtype=jnp.int32)
        s = jax.nn.relu(jnp.einsum('bqhd,bsd->bqhs', iqb.astype(jnp.float32), ik_f))
        score = jnp.einsum('bqhs,bqh->bqs', s, iwb.astype(jnp.float32))
        visible = key_pos[None, :] <= q_pos[:, None]
        score = jnp.where(visible[None], score, -jnp.inf)
        _, idx = lax.top_k(score, topk)
        valid = idx <= q_pos[None, :, None]
        k_sel = jax.vmap(lambda kb, ib: kb[ib])(k, idx)
        v_sel = jax.vmap(lambda vb, ib: vb[ib])(v, idx)
        logits = jnp.einsum('bqcgd,bqncd->bqcgn', qb, k_sel).astype(jnp.float32)
        bucket = t5_bucket(jnp.maximum(q_pos[None, :, None] - idx, 0))
        bias = rel_bias[bucket].reshape(B, Q_BLOCK, topk, KV, G).transpose(0, 1, 3, 4, 2)
        logits = logits + bias.astype(jnp.float32)
        logits = jnp.where(valid[:, :, None, None, :], logits, -1e30)
        p = jax.nn.softmax(logits, axis=-1).astype(v.dtype)
        o = jnp.einsum('bqcgn,bqncd->bqcgd', p, v_sel)
        return o.reshape(B, Q_BLOCK, DSA_HEADS * DSA_HD)

    starts = jnp.arange(nb, dtype=jnp.int32) * Q_BLOCK
    xs = (q.transpose(1, 0, 2, 3, 4, 5), iq.transpose(1, 0, 2, 3, 4),
          iw.transpose(1, 0, 2, 3), starts)
    o = lax.map(block, xs)
    o = o.transpose(1, 0, 2, 3).reshape(B, L, DSA_HEADS * DSA_HD)
    return o * jax.nn.silu(z)

def cross_mixer(q, z, mem_n, w_mem_kv):
    B, L, _ = q.shape
    M = mem_n.shape[1]
    mk, mv = jnp.split(mem_n @ w_mem_kv, 2, axis=-1)
    mk = mk.reshape(B, M, X_HEADS, X_HD)
    mv = mv.reshape(B, M, X_HEADS, X_HD)
    q = q.reshape(B, L, X_HEADS, X_HD) * (X_HD ** -0.5)
    logits = jnp.einsum('bthd,bmhd->bhtm', q, mk).astype(jnp.float32)
    p = jax.nn.softmax(logits, axis=-1).astype(mv.dtype)
    o = jnp.einsum('bhtm,bmhd->bthd', p, mv).reshape(B, L, X_HEADS * X_HD)
    return o * jax.nn.silu(z)

def first_inputs(seed: int = 0) -> dict:
    key = jax.random.key(seed)
    ks = jax.random.split(key, 16)
    D = D_MODEL

    def w(k, shape, fan_in):
        return jax.random.normal(k, shape, jnp.float32) * (fan_in ** -0.5)

    def gain(k, shape):
        return 1.0 + 0.05 * jax.random.normal(k, shape, jnp.float32)

    return {
        "x": jax.random.normal(ks[0], (BATCH, SEQ, D), jnp.float32),
        "mem": jax.random.normal(ks[1], (BATCH, N_MEM, D), jnp.float32),
        "g_pre": gain(ks[2], (DEPTH, D)),
        "g_post": gain(ks[3], (DEPTH, D)),
        "g_mem": gain(ks[4], (DEPTH, D)),
        "w_in": w(ks[5], (DEPTH, D, W_IN_COLS), D),
        "w_gla_a_up": w(ks[6], (DEPTH, GLA_RANK, GLA_HEADS * GLA_DK), GLA_RANK),
        "b_gla_a": 0.1 * jax.random.normal(ks[7], (DEPTH, GLA_HEADS * GLA_DK), jnp.float32),
        "g_gla": gain(ks[8], (DEPTH, GLA_DV)),
        "rel_bias": 0.5 * jax.random.normal(ks[9], (REL_BUCKETS, DSA_HEADS), jnp.float32),
        "w_mem_kv": w(ks[10], (DEPTH, D, 2 * X_HEADS * X_HD), D),
        "w_gla_out": w(ks[11], (DEPTH, GLA_HEADS * GLA_DV, D), GLA_HEADS * GLA_DV),
        "w_dsa_out": w(ks[12], (DEPTH, DSA_HEADS * DSA_HD, D), DSA_HEADS * DSA_HD),
        "w_x_out": w(ks[13], (DEPTH, X_HEADS * X_HD, D), X_HEADS * X_HD),
        "w_o": w(ks[14], (DEPTH, D, D), D),
    }

def first_block(x, mem, g_pre, g_post, g_mem, w_in, w_gla_a_up, b_gla_a, g_gla,
              rel_bias, w_mem_kv, w_gla_out, w_dsa_out, w_x_out, w_o):
    for i in range(DEPTH):
        h = rmsnorm(x, g_pre[i])
        (gq, gk, gv, ga, gz, dq, dk, dv, iq, ik, iw, dz, xq, xz, gates) = split_cols(h @ w_in[i])
        y_gla = gla_mixer(gq, gk, gv, ga, gz, w_gla_a_up[i], b_gla_a[i], g_gla[i])
        y_dsa = dsa_mixer(dq, dk, dv, iq, ik, iw, dz, rel_bias)
        y_mem = cross_mixer(xq, xz, rmsnorm(mem, g_mem[i]), w_mem_kv[i])
        s_gla, s_dsa, s_mem = jnp.split(jax.nn.sigmoid(gates), N_BRANCH, axis=-1)
        merged = (s_gla * (y_gla @ w_gla_out[i]) + s_dsa * (y_dsa @ w_dsa_out[i])
                  + s_mem * (y_mem @ w_x_out[i]))
        x = x + rmsnorm(merged @ w_o[i], g_post[i])
    return x


NORM_EPS = 1e-6
GDN_HEADS = 4
GDN_HEAD_DIM = 128
GDN_WIDTH = GDN_HEADS * GDN_HEAD_DIM
GDN_CONV = 4
GDN_CHUNK = 64
NSA_HEADS = 8
NSA_KV_GROUPS = 2
NSA_GROUP_HEADS = NSA_HEADS // NSA_KV_GROUPS
NSA_HEAD_DIM = 64
NSA_WIDTH = NSA_HEADS * NSA_HEAD_DIM
NSA_KV_WIDTH = NSA_KV_GROUPS * NSA_HEAD_DIM
CMP_BLOCK = 32
CMP_STRIDE = 16
CMP_HIDDEN = 128
SEL_BLOCK = 64
SEL_COUNT = 16
WINDOW = 512
ROPE_THETA = 500000.0
ROPE_DIM = NSA_HEAD_DIM // 4
FORCED_SCORE = 1000.0
NEG_INF = -1e30
FFN_HIDDEN = -(-8 * D_MODEL // (3 * 256)) * 256
IN_SIZES = (3 * GDN_WIDTH, GDN_WIDTH, GDN_HEADS, GDN_HEADS,
            NSA_WIDTH, NSA_KV_WIDTH, NSA_KV_WIDTH, NSA_KV_WIDTH, NSA_KV_WIDTH, NSA_KV_WIDTH, NSA_KV_WIDTH,
            3 * NSA_HEADS, D_MODEL, D_MODEL)
IN_WIDTH = 4 * GDN_WIDTH + 2 * GDN_HEADS + NSA_WIDTH + 6 * NSA_KV_WIDTH + 3 * NSA_HEADS + 2 * D_MODEL


def rms_norm(x, gain):
    x32 = x.astype(jnp.float32)
    y = x32 * lax.rsqrt(jnp.mean(x32 * x32, axis=-1, keepdims=True) + NORM_EPS)
    return (y * gain.astype(jnp.float32)).astype(x.dtype)

def l2_normalize(x):
    return x * lax.rsqrt(jnp.sum(x * x, axis=-1, keepdims=True) + NORM_EPS)

def causal_depthwise_conv(x, w):
    k_len, ch = w.shape
    return lax.conv_general_dilated(x, w[:, None, :].astype(x.dtype), window_strides=(1,),
                                    padding=[(k_len - 1, 0)], dimension_numbers=('NWC', 'WIO', 'NWC'),
                                    feature_group_count=ch)

def partial_rope(x, pos):
    half = ROPE_DIM // 2
    inv_freq = ROPE_THETA ** (-jnp.arange(half, dtype=jnp.float32) / half)
    ang = pos.astype(jnp.float32)[:, None] * inv_freq
    bshape = (pos.shape[0],) + (1,) * (x.ndim - 3) + (half,)
    cos = jnp.cos(ang).reshape(bshape)
    sin = jnp.sin(ang).reshape(bshape)
    x1 = x[..., :half].astype(jnp.float32)
    x2 = x[..., half:ROPE_DIM].astype(jnp.float32)
    rot = jnp.concatenate([x1 * cos - x2 * sin, x2 * cos + x1 * sin], axis=-1).astype(x.dtype)
    return jnp.concatenate([rot, x[..., ROPE_DIM:]], axis=-1)

def gated_delta_rule_chunked(q, k, v, beta, g):
    b_, s_, h_, dk = q.shape
    dv = v.shape[-1]
    c = GDN_CHUNK
    n = s_ // c

    def to_chunks(a):
        return a.reshape(b_, n, c, h_, a.shape[-1]).transpose(0, 3, 1, 2, 4)

    q, k, v = to_chunks(q), to_chunks(k), to_chunks(v)
    beta = beta.reshape(b_, n, c, h_).transpose(0, 3, 1, 2)
    gc = jnp.cumsum(g.reshape(b_, n, c, h_).transpose(0, 3, 1, 2), axis=-1)
    causal = jnp.tril(jnp.ones((c, c), dtype=bool))
    strict = jnp.tril(jnp.ones((c, c), dtype=bool), -1)
    decay = jnp.exp(jnp.where(causal, gc[..., :, None] - gc[..., None, :], -jnp.inf))
    kb = k * beta[..., None]
    a_low = jnp.where(strict, jnp.einsum('bhnid,bhnjd->bhnij', kb, k) * decay, 0.0)
    ia = a_low + jnp.eye(c, dtype=q.dtype)
    u = lax.linalg.triangular_solve(ia, v * beta[..., None], left_side=True, lower=True, unit_diagonal=True)
    w = lax.linalg.triangular_solve(ia, kb * jnp.exp(gc)[..., None], left_side=True, lower=True, unit_diagonal=True)
    qk = jnp.einsum('bhnid,bhnjd->bhnij', q, k) * decay
    qg = q * jnp.exp(gc)[..., None]
    kd = k * jnp.exp(gc[..., -1:] - gc)[..., None]
    g_last = jnp.exp(gc[..., -1])

    def step(state, inp):
        qk_n, qg_n, kd_n, u_n, w_n, gl_n = inp
        v_new = u_n - jnp.einsum('bhcd,bhde->bhce', w_n, state)
        o_n = jnp.einsum('bhcd,bhde->bhce', qg_n, state) + jnp.einsum('bhij,bhje->bhie', qk_n, v_new)
        state = state * gl_n[..., None, None] + jnp.einsum('bhcd,bhce->bhde', kd_n, v_new)
        return state, o_n

    xs = tuple(jnp.moveaxis(a, 2, 0) for a in (qk, qg, kd, u, w, g_last))
    state0 = jnp.zeros((b_, h_, dk, dv), dtype=q.dtype)
    _, o = lax.scan(step, state0, xs)
    return o.transpose(1, 0, 3, 2, 4).reshape(b_, s_, h_, dv)

def compress_blocks(kv, pos_emb, w1, w2):
    s_ = kv.shape[1]
    n_cmp = (s_ - CMP_BLOCK) // CMP_STRIDE + 1
    idx = jnp.arange(n_cmp)[:, None] * CMP_STRIDE + jnp.arange(CMP_BLOCK)[None, :]
    blocks = kv[:, idx] + pos_emb[:, None, :]
    hid = jax.nn.silu(jnp.einsum('bnlgd,ldh->bgnh', blocks, w1))
    return jnp.einsum('bgnh,hd->bgnd', hid, w2)

def native_sparse_attention(q, k_cmp, v_cmp, k_slc, v_slc, k_win, v_win, gates,
                            cmp_pos_k, cmp_w1_k, cmp_w2_k, cmp_pos_v, cmp_w1_v, cmp_w2_v):
    b_, s_, g_, r_, dh = q.shape
    n_cmp = (s_ - CMP_BLOCK) // CMP_STRIDE + 1
    n_blk = s_ // SEL_BLOCK
    n_top = min(SEL_COUNT, n_blk)
    kc = compress_blocks(k_cmp, cmp_pos_k, cmp_w1_k, cmp_w2_k)
    vc = compress_blocks(v_cmp, cmp_pos_v, cmp_w1_v, cmp_w2_v)
    cmp_start = jnp.arange(n_cmp) * CMP_STRIDE
    cmp_end = cmp_start + CMP_BLOCK - 1
    blk_ids = jnp.arange(n_blk)
    sel_start = blk_ids * SEL_BLOCK
    overlap = ((cmp_start[:, None] <= sel_start[None, :] + SEL_BLOCK - 1)
               & (cmp_end[:, None] >= sel_start[None, :])).astype(jnp.float32)

    def to_blocks(a):
        return a.reshape(b_, n_blk, SEL_BLOCK, g_, dh).transpose(0, 3, 1, 2, 4).reshape(b_ * g_ * n_blk, SEL_BLOCK, dh)

    ks_flat = to_blocks(k_slc)
    vs_flat = to_blocks(v_slc)
    base = ((jnp.arange(b_)[:, None] * g_ + jnp.arange(g_)[None, :]) * n_blk)[:, :, None, None]
    pad = ((0, 0), (WINDOW, 0), (0, 0), (0, 0))
    kw_pad = jnp.pad(k_win, pad)
    vw_pad = jnp.pad(v_win, pad)
    span = WINDOW + Q_BLOCK
    q_off = jnp.arange(Q_BLOCK)
    sel_off = jnp.arange(SEL_BLOCK)
    win_off = jnp.arange(span) - WINDOW

    def query_block(qi):
        s0 = qi * Q_BLOCK
        t = s0 + q_off
        qb = lax.dynamic_slice_in_dim(q, s0, Q_BLOCK, axis=1)
        gb = lax.dynamic_slice_in_dim(gates, s0, Q_BLOCK, axis=1)
        vis = cmp_end[None, :] <= t[:, None]
        sc = jnp.einsum('bqgrd,bgnd->bgrqn', qb, kc).astype(jnp.float32)
        p_cmp = jnp.where(vis, jax.nn.softmax(jnp.where(vis, sc, NEG_INF), axis=-1), 0.0)
        o_cmp = jnp.einsum('bgrqn,bgnd->bqgrd', p_cmp.astype(vc.dtype), vc)
        imp = jnp.einsum('bgrqn,nj->bgqj', p_cmp, overlap)
        cur = (t // SEL_BLOCK)[:, None]
        valid = blk_ids[None, :] <= cur
        forced = (blk_ids[None, :] == 0) | (blk_ids[None, :] == cur) | (blk_ids[None, :] == cur - 1)
        score = jnp.where(valid, jnp.where(forced, FORCED_SCORE, imp), -1.0)
        _, top = lax.top_k(score, n_top)
        flat = base + top
        s_list = []
        for s in range(n_top):
            kg = ks_flat[flat[..., s]]
            kpos = top[..., s, None] * SEL_BLOCK + sel_off
            sc_s = jnp.einsum('bqgrd,bgqkd->bgrqk', qb, kg).astype(jnp.float32)
            s_list.append(jnp.where((kpos <= t[:, None])[:, :, None], sc_s, NEG_INF))
        p_sel = jax.nn.softmax(jnp.concatenate(s_list, axis=-1), axis=-1).astype(vs_flat.dtype)
        o_sel = sum(jnp.einsum('bgrqk,bgqkd->bqgrd', p_sel[..., s * SEL_BLOCK:(s + 1) * SEL_BLOCK],
                               vs_flat[flat[..., s]]) for s in range(n_top))
        kw = lax.dynamic_slice_in_dim(kw_pad, s0, span, axis=1)
        vw = lax.dynamic_slice_in_dim(vw_pad, s0, span, axis=1)
        kpos_w = s0 + win_off
        rel = t[:, None] - kpos_w[None, :]
        ok = (rel >= 0) & (rel < WINDOW) & (kpos_w[None, :] >= 0)
        sc_w = jnp.einsum('bqgrd,bkgd->bgrqk', qb, kw).astype(jnp.float32)
        p_w = jax.nn.softmax(jnp.where(ok, sc_w, NEG_INF), axis=-1)
        o_win = jnp.einsum('bgrqk,bkgd->bqgrd', p_w.astype(vw.dtype), vw)
        return gb[..., 0:1] * o_cmp + gb[..., 1:2] * o_sel + gb[..., 2:3] * o_win

    out = lax.map(query_block, jnp.arange(s_ // Q_BLOCK))
    return out.transpose(1, 0, 2, 3, 4, 5).reshape(b_, s_, g_ * r_ * dh)

def hybrid_layer(x, pos, mix_norm_gain, w_in, gdn_conv_w, gdn_a_log, gdn_dt_bias, gdn_out_norm_gain,
                 cmp_pos_k, cmp_w1_k, cmp_w2_k, cmp_pos_v, cmp_w1_v, cmp_w2_v,
                 w_branch_gdn, w_branch_nsa, w_out, ffn_norm_gain, w_gate_up, w_down):
    f32 = jnp.float32
    b_, s_, _ = x.shape
    h = rms_norm(x, mix_norm_gain)
    proj = jnp.einsum('bsd,de->bse', h, w_in)
    split_at = np.cumsum(IN_SIZES)[:-1].tolist()
    (qkv_a, z_a, beta_a, alpha_a, q_b, kc_b, vc_b, ks_b, vs_b, kw_b, vw_b,
     gate_b, merge_a, merge_b) = jnp.split(proj, split_at, axis=-1)

    qkv_a = jax.nn.silu(causal_depthwise_conv(qkv_a, gdn_conv_w))
    q_a, k_a, v_a = [a.reshape(b_, s_, GDN_HEADS, GDN_HEAD_DIM).astype(f32) for a in jnp.split(qkv_a, 3, axis=-1)]
    q_a = l2_normalize(q_a) * (GDN_HEAD_DIM ** -0.5)
    k_a = l2_normalize(k_a)
    beta = jax.nn.sigmoid(beta_a.astype(f32))
    log_decay = -jnp.exp(gdn_a_log.astype(f32)) * jax.nn.softplus(alpha_a.astype(f32) + gdn_dt_bias.astype(f32))
    o_a = gated_delta_rule_chunked(q_a, k_a, v_a, beta, log_decay)
    o_a = (o_a * lax.rsqrt(jnp.mean(o_a * o_a, axis=-1, keepdims=True) + NORM_EPS)
           * gdn_out_norm_gain.astype(f32)
           * jax.nn.silu(z_a.astype(f32).reshape(b_, s_, GDN_HEADS, GDN_HEAD_DIM)))
    o_a = o_a.reshape(b_, s_, GDN_WIDTH).astype(x.dtype)

    q_n = partial_rope(q_b.reshape(b_, s_, NSA_KV_GROUPS, NSA_GROUP_HEADS, NSA_HEAD_DIM), pos) * (NSA_HEAD_DIM ** -0.5)
    kv_shape = (b_, s_, NSA_KV_GROUPS, NSA_HEAD_DIM)
    k_cmp = partial_rope(kc_b.reshape(kv_shape), pos)
    k_slc = partial_rope(ks_b.reshape(kv_shape), pos)
    k_win = partial_rope(kw_b.reshape(kv_shape), pos)
    gates = jax.nn.sigmoid(gate_b.reshape(b_, s_, NSA_KV_GROUPS, NSA_GROUP_HEADS, 3))
    o_b = native_sparse_attention(q_n, k_cmp, vc_b.reshape(kv_shape), k_slc, vs_b.reshape(kv_shape),
                                  k_win, vw_b.reshape(kv_shape), gates,
                                  cmp_pos_k, cmp_w1_k, cmp_w2_k, cmp_pos_v, cmp_w1_v, cmp_w2_v)

    merged = (jax.nn.sigmoid(merge_a) * jnp.einsum('bse,ed->bsd', o_a, w_branch_gdn)
              + jax.nn.sigmoid(merge_b) * jnp.einsum('bse,ed->bsd', o_b, w_branch_nsa))
    x = x + jnp.einsum('bsd,de->bse', merged, w_out)

    h2 = rms_norm(x, ffn_norm_gain)
    gate, up = jnp.split(jnp.einsum('bsd,df->bsf', h2, w_gate_up), 2, axis=-1)
    return x + jnp.einsum('bsf,fd->bsd', jax.nn.silu(gate) * up, w_down)

def second_inputs(seed: int = 0) -> dict:
    key = jax.random.key(seed)
    ks = jax.random.split(key, 24)
    f32 = jnp.float32
    L = DEPTH

    def nrm(k, shape, scale):
        return jax.random.normal(k, shape, f32) * scale

    def gain(k, shape):
        return 1.0 + 0.02 * jax.random.normal(k, shape, f32)

    dt = jnp.exp(jax.random.uniform(ks[5], (L, GDN_HEADS), f32, math.log(1e-3), math.log(1e-1)))
    return {
        'x': nrm(ks[0], (BATCH, SEQ, D_MODEL), 1.0),
        'mix_norm_gain': gain(ks[1], (L, D_MODEL)),
        'w_in': nrm(ks[2], (L, D_MODEL, IN_WIDTH), D_MODEL ** -0.5),
        'gdn_conv_w': nrm(ks[3], (L, GDN_CONV, 3 * GDN_WIDTH), GDN_CONV ** -0.5),
        'gdn_a_log': jnp.log(jax.random.uniform(ks[4], (L, GDN_HEADS), f32, 1.0, 16.0)),
        'gdn_dt_bias': dt + jnp.log(-jnp.expm1(-dt)),
        'gdn_out_norm_gain': gain(ks[6], (L, GDN_HEAD_DIM)),
        'cmp_pos_k': nrm(ks[7], (L, CMP_BLOCK, NSA_HEAD_DIM), 0.02),
        'cmp_w1_k': nrm(ks[8], (L, CMP_BLOCK, NSA_HEAD_DIM, CMP_HIDDEN), (CMP_BLOCK * NSA_HEAD_DIM) ** -0.5),
        'cmp_w2_k': nrm(ks[9], (L, CMP_HIDDEN, NSA_HEAD_DIM), CMP_HIDDEN ** -0.5),
        'cmp_pos_v': nrm(ks[10], (L, CMP_BLOCK, NSA_HEAD_DIM), 0.02),
        'cmp_w1_v': nrm(ks[11], (L, CMP_BLOCK, NSA_HEAD_DIM, CMP_HIDDEN), (CMP_BLOCK * NSA_HEAD_DIM) ** -0.5),
        'cmp_w2_v': nrm(ks[12], (L, CMP_HIDDEN, NSA_HEAD_DIM), CMP_HIDDEN ** -0.5),
        'w_branch_gdn': nrm(ks[13], (L, GDN_WIDTH, D_MODEL), GDN_WIDTH ** -0.5),
        'w_branch_nsa': nrm(ks[14], (L, NSA_WIDTH, D_MODEL), NSA_WIDTH ** -0.5),
        'w_out': nrm(ks[15], (L, D_MODEL, D_MODEL), D_MODEL ** -0.5),
        'ffn_norm_gain': gain(ks[16], (L, D_MODEL)),
        'w_gate_up': nrm(ks[17], (L, D_MODEL, 2 * FFN_HIDDEN), D_MODEL ** -0.5),
        'w_down': nrm(ks[18], (L, FFN_HIDDEN, D_MODEL), FFN_HIDDEN ** -0.5),
        'final_norm_gain': gain(ks[19], (D_MODEL,)),
    }

def second_block(x, mix_norm_gain, w_in, gdn_conv_w, gdn_a_log, gdn_dt_bias, gdn_out_norm_gain,
              cmp_pos_k, cmp_w1_k, cmp_w2_k, cmp_pos_v, cmp_w1_v, cmp_w2_v,
              w_branch_gdn, w_branch_nsa, w_out, ffn_norm_gain, w_gate_up, w_down, final_norm_gain):
    pos = jnp.arange(x.shape[1])
    for layer in range(DEPTH):
        x = hybrid_layer(x, pos, mix_norm_gain[layer], w_in[layer], gdn_conv_w[layer], gdn_a_log[layer],
                         gdn_dt_bias[layer], gdn_out_norm_gain[layer],
                         cmp_pos_k[layer], cmp_w1_k[layer], cmp_w2_k[layer],
                         cmp_pos_v[layer], cmp_w1_v[layer], cmp_w2_v[layer],
                         w_branch_gdn[layer], w_branch_nsa[layer], w_out[layer],
                         ffn_norm_gain[layer], w_gate_up[layer], w_down[layer])
    return rms_norm(x, final_norm_gain)


def setup_inputs(seed=0):
    out = dict(first_inputs(seed))
    for name, value in second_inputs(seed + 1).items():
        if name != "x":
            out[name + "_2"] = value
    return out


def reference(
    x, mem, g_pre, g_post, g_mem, w_in, w_gla_a_up, b_gla_a, g_gla, rel_bias, w_mem_kv,
    w_gla_out, w_dsa_out, w_x_out, w_o, mix_norm_gain_2, w_in_2, gdn_conv_w_2, gdn_a_log_2,
    gdn_dt_bias_2, gdn_out_norm_gain_2, cmp_pos_k_2, cmp_w1_k_2, cmp_w2_k_2, cmp_pos_v_2,
    cmp_w1_v_2, cmp_w2_v_2, w_branch_gdn_2, w_branch_nsa_2, w_out_2, ffn_norm_gain_2,
    w_gate_up_2, w_down_2, final_norm_gain_2,
):
    x = first_block(
        x, mem, g_pre, g_post, g_mem, w_in, w_gla_a_up, b_gla_a, g_gla, rel_bias, w_mem_kv,
        w_gla_out, w_dsa_out, w_x_out, w_o,
    )
    return second_block(
        x, mix_norm_gain_2, w_in_2, gdn_conv_w_2, gdn_a_log_2, gdn_dt_bias_2,
        gdn_out_norm_gain_2, cmp_pos_k_2, cmp_w1_k_2, cmp_w2_k_2, cmp_pos_v_2, cmp_w1_v_2,
        cmp_w2_v_2, w_branch_gdn_2, w_branch_nsa_2, w_out_2, ffn_norm_gain_2, w_gate_up_2,
        w_down_2, final_norm_gain_2,
    )


_drawn_inputs = setup_inputs


def setup_inputs(seed=0):
    import zlib

    import numpy as np

    out = dict(_drawn_inputs(seed))
    spreads = {}
    factors = {'g_mem': 8.0,
     'mix_norm_gain_2': 6.759,
     'gdn_out_norm_gain_2': 8.0,
     'cmp_pos_k_2': 64.0,
     'cmp_pos_v_2': 64.0,
     'ffn_norm_gain_2': 16.561,
     'b_gla_a': 4.151,
     'g_gla': 3.576}
    for name, (base, spread) in spreads.items():
        noise = np.random.default_rng([zlib.crc32(name.encode()), seed]).standard_normal(out[name].shape)
        drawn = base * np.exp(spread * noise) if base else spread * noise
        out[name] = jnp.asarray(drawn.astype(out[name].dtype))
    for name, factor in factors.items():
        out[name] = (out[name] * factor).astype(out[name].dtype)
    return out
```

```python
import math
from contextlib import ExitStack

import numpy as np

import concourse.bass as bass
from concourse import mybir

D = 1024
S = 256
KT = D // 128
TT = S // 128
H1, DK, DV, RANK = 4, 128, 256, 16
CH = 64
NCH = S // CH
DH = 8
IDX_H, IDX_D = 8, 64
TOPK = min(256, S // 4)
XH = 4
W1_OFF = dict(gq=0, gk=512, gv=1024, ga=2048, gz=2064, dq=3088, dk=4112, dv=4368, iq=4624, ik=5136,
              iw=5200, dz=5208, xq=6232, xz=7256, sg=8280)
W2_OFF = dict(qkv=0, z=1536, beta=2048, alpha=2052, q=2056, kc=2568, vc=2696, ks=2824, vs=2952,
              kw=3080, vw=3208, gate=3336, ma=3360, mb=4384)
FFN = -(-8 * D // (3 * 256)) * 256
FT = FFN // 128
CMP_L, CMP_S = 32, 16
NCMP = (S - CMP_L) // CMP_S + 1
NEG = -1e30
TAKEN = -3e38
EPS = 1e-6
NSLOT = 5
ARENA = 53200
FFN_AT = 24800

CONST = {}


def _const_columns():
    at = 0
    for name, width in (("ident", 128), ("keep", S), ("chunk", 128), ("lev", 6 * 128),
                        ("diag3", 384), ("rope", 128), ("cos", S), ("sin", S), ("selg", 256),
                        ("ones", 1), ("rowsel", 1024), ("rowscale", 1), ("bucket", 383),
                        ("cneg", 2 * 16), ("cvis", 2 * 16), ("mhalf", 1)):
        CONST[name] = (at, width)
        at += width
    return at


NCONST = _const_columns()


def shape_constants():
    c = np.zeros((128, NCONST), np.float32)

    def put(name, value, rows=128):
        at, width = CONST[name]
        c[:rows, at:at + width] = np.asarray(value, np.float32).reshape(rows, width)

    p = np.arange(128)[:, None]
    f = np.arange(128)[None, :]
    same = (p // CH) == (f // CH)
    put("ident", p == f)
    put("keep", np.broadcast_to(np.arange(S) % CH != 0, (128, S)))
    put("chunk", same & (p <= f))
    lev = []
    for level in range(6):
        b = 1 << level
        lev.append(((p // (2 * b)) == (f // (2 * b))) & ((p // b) % 2 == 1) & ((f // b) % 2 == 0))
    put("lev", np.concatenate(lev, 1))
    diag = np.where(f <= p, 0.0, NEG)
    put("diag3", np.concatenate([diag, np.zeros((128, 128)), diag], 1))
    rot = np.zeros((128, 128), np.float32)
    cos = np.ones((128, S), np.float32)
    sin = np.zeros((128, S), np.float32)
    freq = np.float32(500000.0) ** (-np.arange(8, dtype=np.float32) / np.float32(8))
    ang = (np.arange(S, dtype=np.float32)[:, None] * freq.astype(np.float32)[None, :]).astype(np.float32)
    for g in range(2):
        for i in range(8):
            a, b = 64 * g + i, 64 * g + 8 + i
            cos[a] = cos[b] = np.cos(ang[:, i])
            sin[a] = sin[b] = np.sin(ang[:, i])
            rot[b, a] = -1.0
            rot[a, b] = 1.0
    put("rope", rot)
    put("cos", cos)
    put("sin", sin)
    selg = np.zeros((128, 2, 128), np.float32)
    for g in range(2):
        for d in range(64):
            selg[64 * g + d, g, d] = 1
            selg[64 * g + d, g, 64 + d] = 1
    put("selg", selg)
    put("ones", np.ones((128, 1)))
    rowsel = np.zeros((128, 8, 128), np.float32)
    for i in range(8):
        rowsel[i, i, :] = 1
    put("rowsel", rowsel)
    rs = np.zeros((128, 1), np.float32)
    rs[0:4] = 0.5 * 128 ** -0.5
    rs[4:8] = 0.5
    put("rowscale", rs)
    dist = np.maximum(255 - np.arange(383), 0)
    d1 = np.maximum(dist, 1).astype(np.float32)
    large = 16 + (np.log(d1 / np.float32(16)) / np.float32(math.log(128 / 16)) * np.float32(16)).astype(np.int32)
    bucket = np.where(dist < 16, dist, np.minimum(large, 31))
    put("bucket", np.arange(32)[:, None] == bucket[None, :], 32)
    t = np.arange(128)[:, None, None] + 128 * np.arange(2)[None, :, None]
    end = (np.arange(16) * CMP_S + CMP_L - 1)[None, None, :]
    vis = (end <= t) & (np.arange(16) < NCMP)[None, None, :]
    put("cneg", np.where(vis, 0.0, NEG))
    put("cvis", vis)
    put("mhalf", np.full((128, 1), -0.5))
    return c


def build(nc, A, consts, out):
    F = mybir.dt.float32
    U32 = mybir.dt.uint32
    ALU = mybir.AluOpType
    ACT = mybir.ActivationFunctionType
    X = mybir.AxisListType.X
    mm = nc.tensor.matmul
    act = nc.scalar.activation
    stt = nc.vector.scalar_tensor_tensor
    tsc = nc.vector.tensor_scalar
    tt_ = nc.vector.tensor_tensor
    ctx = ExitStack()
    with ctx:
        signals = {}

        def signal(name):
            if name not in signals:
                signals[name] = ctx.enter_context(nc.semaphore(name))
            return signals[name]

        R = mybir.dt.float32r
        shared = ctx.enter_context(nc.sbuf_tensor("shared", [128, FFN_AT], F))
        with ExitStack() as over:
            w_hi, w_lo = (over.enter_context(nc.sbuf_tensor(n, [128, 2, 2048], R)) for n in ("w_hi", "w_lo"))
            h_hi, h_lo = (over.enter_context(nc.sbuf_tensor(n, [128, KT, S], R)) for n in ("h_hi", "h_lo"))
            f_hi, f_lo = (over.enter_context(nc.sbuf_tensor(n, [128, FT, S], R)) for n in ("f_hi", "f_lo"))
        arena = ctx.enter_context(nc.sbuf_tensor("arena", [128, ARENA - FFN_AT], F))
        banks = [ctx.enter_context(nc.psum_tensor(f"bank{b}", [128, 512], F)) for b in range(8)]
        bank_full = [signal(f"bank_full{b}") for b in range(8)]
        bank_read = [signal(f"bank_read{b}") for b in range(8)]
        slot_loaded = [signal(f"slot_loaded{i}") for i in range(NSLOT)]
        bias_rows = nc.dram_tensor("bias_rows", (DH, 128, 383), F, kind="Internal").ap()
        end = [0]

        def region(n):
            end[0] += n
            assert end[0] <= ARENA, end[0]
            return end[0] - n

        def flat(off, n, rows=128):
            if off < FFN_AT:
                assert off + n <= FFN_AT
                return shared[0:rows, off:off + n]
            return arena[0:rows, off - FFN_AT:off - FFN_AT + n]

        def tiled(off, a, b):
            return flat(off, a * b).rearrange("p (a b) -> p a b", a=a)

        cst_at = region(NCONST)

        def const(name):
            a, w = CONST[name]
            return flat(cst_at + a, w)

        ident = const("ident")
        mhalf = const("mhalf")
        diag3 = const("diag3")
        rowsel = const("rowsel").rearrange("p (a b) -> p a b", a=8)
        ring = tiled(region(NSLOT * 2048), NSLOT, 2048)
        xres = tiled(region(TT * D), TT, D)
        xn_at = region(TT * D)
        xn = tiled(xn_at, TT, D)
        hT = tiled(region(KT * S), KT, S)
        stat = flat(region(128), 128)
        par = flat(region(136), 136)
        gain = {"x": par[:, 0:8], "m": par[:, 8:16], "y": par[:, 16:24], "f": par[:, 24:32]}
        g_gla, b_gla = par[:, 32:34], par[:, 34:38]
        conv_w = par[:, 38:86].rearrange("p (j t) -> p t j", t=12)
        g_gdn = par[:, 86:87]
        a_log, dt_bias, a_pos = (par[0:4, i:i + 1] for i in (119, 120, 121))
        cmp_pos = (par[:, 87:103], par[:, 103:119])
        rel = par[0:32, 122:130]
        g_gla_half, g_gdn_half = par[:, 130:132], par[:, 132:133]
        sumsq, rstd, neg_max, p_sum, p_inv, var = (stat[:, 16 * i:16 * i + 16] for i in range(6))
        decay1 = stat[:, 96:112]
        prob_at = region(3 * 512)
        prob = tiled(prob_at, 3, 512)
        probT_at = region(3 * 512)
        probT = tiled(probT_at, 3, 512)
        nprobT = [flat(probT_at + 384 * i, 384) for i in range(4)]
        tnh = tiled(region(2 * 512), 2, 512)
        par_rows = tnh[:, 0, 0:128]
        both_end = FFN_AT
        assert end[0] <= FFN_AT
        end[0] = FFN_AT
        assert FFN_AT + 8192 + 4096 + 2 * FT * S <= ARENA

        memT_at = region(KT * S)
        memT = tiled(memT_at, KT, S)
        xq_at, mk_at, mv_at = region(8 * S), region(8 * S), region(8 * S)
        xq, mk, mv = tiled(xq_at, 8, S), tiled(mk_at, 8, S), tiled(mv_at, TT, D)
        memn = mv
        state = (flat(memT_at, 1024), flat(memT_at + 1024, 1024), flat(mk_at + 1024, 1024))
        cumlog, expo = tiled(xq_at, 4, S), tiled(xq_at + 1024, 4, S)
        k_d = tiled(mk_at, 4, S)
        kt_tok, expo_last = tiled(mv_at, 8, 128), flat(mv_at + 1024, 1024)
        gq_at = region(4 * S)
        gk_at = region(4 * S)
        gq, gk = tiled(gq_at, 4, S), tiled(gk_at, 4, S)
        toep = tiled(gq_at, DH, 256)
        gv_at = region(TT * D)
        gv = tiled(gv_at, TT, D)
        assert end[0] == FFN_AT + 12288
        dq_at = region(8 * S)
        dq = tiled(dq_at, 8, S)
        merged = tiled(dq_at, KT, S)
        dkv_at = region(D)
        dk, dv = tiled(dkv_at, 2, S), tiled(dkv_at + 2 * S, TT, S)
        g_post = flat(dkv_at, D)
        iq = tiled(region(4 * S), 4, S)
        ikT, gaT = flat(region(S), S), flat(region(S), S, 16)
        iw = tiled(region(16), TT, 8)
        zg_at = region(8 * S)
        zd_at = region(8 * S)
        zg, zd, zx = tiled(zg_at, 8, S), tiled(zd_at, 8, S), tiled(region(8 * S), 8, S)
        bias_out = tiled(zg_at, DH, 383)
        relb = flat(prob_at, 1024, 32).rearrange("p (h m) -> p h m", h=DH)
        w_up = flat(region(512), 512, 16)
        relu = tiled(region(2 * 512), 2, 512)
        score = flat(region(384), 384)
        pen = flat(region(384), 384)
        bias_pen = tiled(region(2 * 384), 2, 384)
        top8 = flat(region(8), 8)
        attT = tiled(region(1024), 8, 128)
        g_out = xn

        end[0] = both_end
        raw_at = region(12 * (S + 3))
        raw = tiled(raw_at, 12, S + 3)
        cv_at = region(12 * S)
        cv = tiled(cv_at, 12, S)
        ns = tiled(region(8 * S), 8, S)
        v_tok = tiled(region(TT * S), TT, S)
        z2 = tiled(region(4 * S), 4, S)
        ma, mb = tiled(region(8 * S), 8, S), tiled(region(8 * S), 8, S)
        rows_at = region(7 * S)
        row_beta, row_g, row_gc, row_last, row_a, row_b = (flat(rows_at + i * S, S, 4) for i in range(6))
        norm_rows = flat(rows_at + 6 * S, S, 8)
        egc = tiled(region(4 * S), 4, S)
        cols = tiled(region(64), TT, 32)
        gate_tok = tiled(region(48), TT, 24)
        kbe, kdt, vb = (tiled(region(1024), 8, 128) for _ in range(3))
        nA, qkT = tiled(region(1024), 8, 128), tiled(region(1024), 8, 128)
        Tm, TmT, zst = (tiled(region(1024), 8, 128) for _ in range(3))
        nAm = (tiled(region(1024), 8, 128), tiled(region(1024), 8, 128))
        gstate = [flat(cv_at + 512 * i, 512) for i in range(3)]
        u_tok, wT, v_new = zst, nAm[0], nAm[1]
        sq = tiled(raw_at, 8, S)
        cblk_at = raw_at + 8 * S
        cblk = [flat(cblk_at + 480 * i, 480).rearrange("p (j n) -> p j n", j=16) for i in range(2)]
        hid = flat(cblk_at + 960, 64)
        ftmp = tiled(raw_at, 2, 512)
        oT = tiled(raw_at + 1024, 4, S)
        norm_cols = flat(region(16), 16)
        kcT, vcn = flat(region(16), 16), flat(region(128), 128, 16)
        w2k, w2v = flat(region(64), 64), flat(region(64), 64)
        pc = tiled(region(2 * 128), TT, 128)
        pcT = flat(xn_at, 8 * S, 16)
        g_fin = hT.rearrange("p a b -> p (a b)")[:, 0:D]
        w1, w2 = A["w_in"][0], A["w_in_2"][0]

        def rows_of(w, k0=0, k1=None):
            v = w.rearrange("(k p) c -> p k c", p=128)
            return v[:, k0:k1 if k1 is not None else v.shape[1], :]

        def piece(w, c0, n, at=0, k0=0, k1=None):
            v = rows_of(w, k0, k1)
            return (v[:, :, c0:c0 + n], v.shape[1], at)

        units = {}

        def unit(name, *pieces, width=256):
            units[name] = (pieces, width)

        def units_of(name, w, c0, n, first=0):
            for j in range(n):
                unit(f"{name}{first + j}", piece(w, c0 + 256 * j, 256))

        unit("small", piece(w1, W1_OFF["ik"], 64, 0), piece(w1, W1_OFF["ik"], 64, 64),
             piece(w1, W1_OFF["ga"], RANK, 128), piece(w1, W1_OFF["iw"], 8, 144))
        units_of("iq", w1, W1_OFF["iq"], 2)
        units_of("mk", A["w_mem_kv"][0], 0, 4)
        units_of("mv", A["w_mem_kv"][0], D, 4)
        units_of("xq", w1, W1_OFF["xq"], 4)
        units_of("zx", w1, W1_OFF["xz"], 4)
        for j in range(2):
            units_of("gq", w1, W1_OFF["gq"] + 256 * j, 1, j)
        for j in range(2):
            units_of("gk", w1, W1_OFF["gk"] + 256 * j, 1, j)
        units_of("gv", w1, W1_OFF["gv"], 4)
        units_of("dk", w1, W1_OFF["dk"], 1)
        units_of("dv", w1, W1_OFF["dv"], 1)
        units_of("dq", w1, W1_OFF["dq"], 4)
        units_of("zg", w1, W1_OFF["gz"], 4)
        units_of("zd", w1, W1_OFF["dz"], 4)
        for j in range(4):
            for b, w in enumerate(("w_gla_out", "w_dsa_out", "w_x_out")):
                units_of(f"sg{b}", w1, W1_OFF["sg"] + D * b + 256 * j, 1, j)
                units_of(f"bo{b}", A[w][0], 256 * j, 1, j)
        units_of("wo", A["w_o"][0], 0, 4)

        unit("beta", piece(w2, W2_OFF["beta"], 8, 0), piece(w2, W2_OFF["gate"], 24, 8))
        units_of("c", w2, W2_OFF["qkv"], 6)
        unit("kcks", piece(w2, W2_OFF["kc"], 128), piece(w2, W2_OFF["ks"], 128, 128))
        unit("kwvc", piece(w2, W2_OFF["kw"], 128), piece(w2, W2_OFF["vc"], 128, 128))
        unit("vsvw", piece(w2, W2_OFF["vs"], 128), piece(w2, W2_OFF["vw"], 128, 128))
        for j in range(2):
            unit(f"nq{j}", *(piece(w2, W2_OFF["q"] + 256 * g + 64 * (2 * j + r), 64, 128 * r + 64 * g)
                             for r in range(2) for g in range(2)))
        for i, (w, name) in enumerate(((A["cmp_w1_k_2"][0], "w1k"), (A["cmp_w1_v_2"][0], "w1v"))):
            units[name] = (w, None)
        units_of("z", w2, W2_OFF["z"], 2)
        units_of("ma", w2, W2_OFF["ma"], 4)
        units_of("mb", w2, W2_OFF["mb"], 4)
        bg = A["w_branch_gdn_2"][0]
        bn = A["w_branch_nsa_2"][0]
        for j in range(2):
            unit(f"bg{j}", piece(bg, 512 * j, 512), width=512)
            units[f"bn{j}"] = (bn, 512 * j)
        units_of("w2o", A["w_out_2"][0], 0, 4)
        gu = A["w_gate_up_2"][0]
        for j in range(FT):
            unit(f"gu{j}", piece(gu, 128 * j, 128), piece(gu, FFN + 128 * j, 128, 128))
        for c in range(4):
            for q, k0 in enumerate(range(0, FT, 8)):
                unit(f"wd{c}{q}", piece(A["w_down_2"][0], 256 * c, 256, 0, k0, min(k0 + 8, FT)))

        def dma_count(name):
            special = name.startswith("bn") or name in ("w1k", "w1v")
            return 2 if special else len(units[name][0])

        turns = {}
        order = []
        freed_by = {}

        def full(name):
            n = turns[name]
            return bank_full[n % 8], n // 8 + 1

        def read(name):
            n = turns[name]
            return bank_read[n % 8], n // 8 + 1

        def bank_of(name):
            return banks[turns[name] % 8]

        def index_heads(t, j):
            if t == 0:
                return [2 * hh + j for hh in range(4)]
            return [4 * (j // 2) + j % 2 + 2 * hh for hh in range(2)]

        ffn_units = [f"gu{j}" for j in range(FT)] + [f"wd{c}{q}" for c in range(4) for q in range(-(-FT // 8))]
        split_units = [f"sg{b}{j}" for j in range(4) for b in range(3)] + ffn_units
        nsg = 12
        loaded = {}

        def ffn_tiles(name):
            return 8 if name[0] in "gs" else min(8, FT - 8 * int(name[3]))

        def ffn_free(n):
            name = split_units[n]
            if name[0] in "gs":
                return full(name)
            return (signal("down_part"), 2 * int(name[2]) + int(name[3]) + 1) if name[3] < "2" else full(name[:3])

        block = ctx.enter_context(nc.Block())

        @block.tensor
        def _(pe):
            loads = [0] * NSLOT

            def open_bank(name):
                n = len(turns)
                turns[name] = n
                if n >= 8:
                    pe.wait_ge(bank_read[n % 8], n // 8)
                return banks[n % 8]

            def done(name, ins):
                ins.then_inc(full(name)[0], 1)

            def unit_here(name, k=8):
                i = len(order) % NSLOT
                order.append(name)
                loads[i] += 16 * dma_count(name)
                loaded[name] = (slot_loaded[i], loads[i])
                if name in split_units:
                    n = split_units.index(name)
                    freed_by[name] = ("w_split", n + 1)
                    pe.wait_ge(signal("w_split"), n + 1)
                    return tuple(w[:, n % 2, :].rearrange("p (k c) -> p k c", k=k) for w in (w_hi, w_lo))
                pe.wait_ge(slot_loaded[i], loads[i])
                return ring[:, i, :].rearrange("p (k c) -> p k c", k=k)

            def project_channels(name, x, k=KT, width=256, unit=None):
                w = unit_here(unit or name, 2048 // width)
                for half in range(width // 256):
                    title = name + ("ab"[half] if width > 256 else "")
                    bank = open_bank(title)
                    for c in range(2):
                        for i in range(k):
                            at = 256 * half + 128 * c
                            ins = mm(bank[:, 256 * c:256 * c + 256], w[:, i, at:at + 128], x[:, i, :],
                                     start=i == 0, stop=i == k - 1)
                    done(title, ins)
                freed_by[name] = title

            def project_tokens(name, x):
                w = unit_here(name)
                bank = open_bank(name)
                for t in range(TT):
                    for i in range(KT):
                        ins = mm(bank[:, 256 * t:256 * t + 256], x[:, i, 128 * t:128 * t + 128], w[:, i, :],
                                 start=i == 0, stop=i == KT - 1)
                done(name, ins)
                freed_by[name] = name

            def transpose_tokens(tag, src):
                pe.wait_ge(signal(f"scaled_{tag}"), 1)
                for j in range(4):
                    bank = open_bank(f"T{tag}{j}")
                    for kk in range(2):
                        for t in range(TT):
                            k = 2 * j + kk
                            ins = nc.tensor.transpose(bank[:, 256 * kk + 128 * t:256 * kk + 128 * t + 128],
                                                      src[:, t, 128 * k:128 * k + 128], ident)
                    done(f"T{tag}{j}", ins)

            pe.wait_ge(signal("params"), 16 * 14)
            pe.wait_ge(signal("consts"), 16)
            bank = open_bank("par")
            done("par", nc.tensor.transpose(bank[:, 0:119], par_rows[0:119, :], ident[0:119, 0:119]))
            pe.wait_ge(signal("relb_ready"), 1)
            for h in range(DH):
                bank = open_bank(f"tb{h}")
                done(f"tb{h}", mm(bank[:, 0:383], relb[:, h, :], const("bucket")[0:32, :], start=True, stop=True))
            transpose_tokens("x", xn)
            pe.wait_ge(*read("Tx3"))
            w = unit_here("small")
            bank = open_bank("ikga")
            for i in range(KT):
                mm(bank[:, 0:256], w[:, i, 0:128], hT[:, i, :], start=i == 0, stop=i == KT - 1)
            for i in range(KT):
                ins = mm(bank[0:RANK, 256:512], w[:, i, 128:144], hT[:, i, :], start=i == 0, stop=i == KT - 1)
            done("ikga", ins)
            bank = open_bank("iw")
            for t in range(TT):
                for i in range(KT):
                    ins = mm(bank[:, 8 * t:8 * t + 8], hT[:, i, 128 * t:128 * t + 128], w[:, i, 144:152],
                             start=i == 0, stop=i == KT - 1)
            done("iw", ins)
            freed_by["small"] = "iw"
            for j in range(2):
                project_channels(f"iq{j}", hT)
            transpose_tokens("m", memn)
            pe.wait_ge(*read("ikga"))
            pe.wait_ge(*read("iq1"))
            for t in range(TT):
                n, per = (128, 4) if t == 0 else (256, 2)
                for j in range(IDX_H // per):
                    bank = open_bank(f"is{t}{j}")
                    for hh, h in enumerate(index_heads(t, j)):
                        r = 64 * (h % 2)
                        ins = mm(bank[:, n * hh:n * hh + n], iq[r:r + 64, h // 2, 128 * t:128 * t + 128],
                                 ikT[r:r + 64, 0:n], start=True, stop=True)
                    done(f"is{t}{j}", ins)
            pe.wait_ge(*read("Tm3"))
            for j in range(4):
                project_channels(f"mk{j}", memT)
            for j in range(4):
                project_tokens(f"mv{j}", memT)
            for j in range(4):
                project_channels(f"xq{j}", hT)
            for j in range(4):
                project_channels(f"zx{j}", hT)

            def cross_logits(h):
                pe.wait_ge(*read(f"mk{h}"))
                pe.wait_ge(*read(f"xq{h}"))
                bank = open_bank(f"xl{h}")
                for t in range(TT):
                    for c in range(2):
                        ins = mm(bank[:, 256 * t:256 * t + 256], xq[:, 2 * h + c, 128 * t:128 * t + 128],
                                 mk[:, 2 * h + c, :], start=c == 0, stop=c == 1)
                done(f"xl{h}", ins)

            def cross_transposes(h):
                pe.wait_ge(signal("xprob"), h + 1)
                bank = open_bank(f"xp{h}")
                for m in range(2):
                    for t in range(TT):
                        ins = nc.tensor.transpose(bank[:, 256 * m + 128 * t:256 * m + 128 * t + 128],
                                                  prob[:, h % 3, 256 * t + 128 * m:256 * t + 128 * m + 128], ident)
                done(f"xp{h}", ins)

            def cross_out(h):
                pe.wait_ge(*read(f"mv{h}"))
                pe.wait_ge(*read(f"xp{h}"))
                bank = open_bank(f"xo{h}")
                for c in range(2):
                    for m in range(2):
                        at = 256 * h + 128 * c
                        ins = mm(bank[:, 256 * c:256 * c + 256], mv[:, m, at:at + 128],
                                 probT[:, h % 3, 256 * m:256 * m + 256], start=m == 0, stop=m == 1)
                done(f"xo{h}", ins)

            cross_logits(0)
            cross_logits(1)
            project_channels("gq0", hT)
            cross_logits(2)
            project_channels("gq1", hT)
            cross_transposes(0)
            cross_logits(3)
            project_channels("gk0", hT)
            cross_out(0)
            cross_transposes(1)
            project_channels("gk1", hT)
            for j in range(2):
                bank = open_bank(f"ax{j}")
                for hh in range(2):
                    h = 2 * j + hh
                    ins = mm(bank[:, 256 * hh:256 * hh + 256], w_up[:, 128 * h:128 * h + 128], gaT,
                             start=True, stop=True)
                done(f"ax{j}", ins)
            cross_out(1)
            cross_transposes(2)
            project_tokens("gv0", hT)
            cross_out(2)
            cross_transposes(3)
            project_tokens("gv1", hT)
            cross_out(3)
            for j in (2, 3):
                project_tokens(f"gv{j}", hT)
            project_channels("dk0", hT)
            project_tokens("dv0", hT)
            for j in range(4):
                project_channels(f"dq{j}", hT)

            pe.wait_ge(signal("gla_kd"), 1)
            for j in range(TT):
                bank = open_bank(f"at{j}")
                for h in range(H1):
                    ins = mm(bank[:, 128 * h:128 * h + 128], k_d[:, h, 128 * j:128 * j + 128],
                             gq[:, h, 128 * j:128 * j + 128], start=True, stop=True)
                done(f"at{j}", ins)
            pe.wait_ge(signal("gla_kt"), 1)
            for j in range(TT):
                bank = open_bank(f"kt{j}")
                for h in range(H1):
                    ins = nc.tensor.transpose(bank[:, 128 * h:128 * h + 128], gk[:, h, 128 * j:128 * j + 128], ident)
                done(f"kt{j}", ins)
            project_channels("zg0", hT)
            project_channels("zg1", hT)
            for c in range(NCH - 1):
                r = 64 * (c % 2)
                pe.wait_ge(*read(f"kt{c // 2}"))
                for j in range(2):
                    bank = open_bank(f"kv{c}{j}")
                    for hh in range(2):
                        h = 2 * j + hh
                        ins = mm(bank[:, 256 * hh:256 * hh + 256], kt_tok[r:r + 64, 4 * (c // 2) + h, :],
                                 gv[r:r + 64, c // 2, 256 * h:256 * h + 256], start=True, stop=True)
                    done(f"kv{c}{j}", ins)
            project_channels("zg2", hT)
            project_channels("zg3", hT)
            for h in range(H1):
                if h == 0:
                    pe.wait_ge(*read("at1"))
                    pe.wait_ge(*read("kv21"))
                bank = open_bank(f"og{h}")
                for t in range(TT):
                    o = bank[:, 256 * t:256 * t + 256]
                    mm(o, attT[:, 4 * t + h, :], gv[:, t, 256 * h:256 * h + 256], start=True, stop=True)
                    for c in (2 * t, 2 * t + 1):
                        if c > 0:
                            r = 64 * (c % 2)
                            ins = mm(o[r:r + 64, :], gq[:, h, 64 * c:64 * c + 64],
                                     state[c - 1][:, 256 * h:256 * h + 256], start=False, stop=True,
                                     skip_group_check=True)
                done(f"og{h}", ins)
            for j in range(4):
                project_channels(f"zd{j}", hT)
            for h in range(H1):
                pe.wait_ge(*read(f"og{h}"))
                bank = open_bank(f"yt{h}")
                for c in range(2):
                    for t in range(TT):
                        at = 256 * h + 128 * c
                        ins = nc.tensor.transpose(bank[:, 256 * c + 128 * t:256 * c + 128 * t + 128],
                                                  g_out[:, t, at:at + 128], ident)
                done(f"yt{h}", ins)

            def causal_logits(name, qT, kT_, r):
                bank = open_bank(name)
                mm(bank[:, 0:128], qT[r[0]:r[1], 0:128], kT_[r[0]:r[1], 0:128], start=True, stop=True)
                done(name, mm(bank[:, 128:384], qT[r[0]:r[1], 128:256], kT_[r[0]:r[1], :], start=True, stop=True))

            def causal_transposes(name, i):
                bank = open_bank(name)
                for a, b in ((0, 0), (128, 128), (256, 256)):
                    ins = nc.tensor.transpose(bank[:, b:b + 128], prob[:, i, a:a + 128], ident)
                done(name, ins)

            def sparse_out(j):
                bank = open_bank(f"do{j}")
                for hh in range(2):
                    h = 2 * j + hh
                    g = h // 4
                    pe.wait_ge(*read(f"dp{h}"))
                    o = bank[:, 256 * hh:256 * hh + 256]
                    mm(o, dv[:, 0, 128 * g:128 * g + 128], probT[:, h % 3, 0:256], start=True, stop=True)
                    ins = mm(o[:, 128:256], dv[:, 1, 128 * g:128 * g + 128], probT[:, h % 3, 256:384],
                             start=False, stop=True, skip_group_check=True)
                done(f"do{j}", ins)

            pe.wait_ge(*read("dk0"))
            pe.wait_ge(*read("dv0"))
            pe.wait_ge(*read("dq3"))
            for h in range(DH + 2):
                if h < DH:
                    causal_logits(f"dl{h}", dq[:, h, :], dk[:, h // 4, :], (0, 128))
                if h >= 2:
                    pe.wait_ge(signal("dprob"), h - 1)
                    causal_transposes(f"dp{h - 2}", (h - 2) % 3)
                    if h % 2 == 1:
                        sparse_out((h - 3) // 2)
            def split_channels(name):
                wh, wl = unit_here(name)
                bank = open_bank(name)
                for c in range(2):
                    s = slice(128 * c, 128 * c + 128)
                    o = bank[:, 256 * c:256 * c + 256]
                    for i in range(KT):
                        mm(o, wh[:, i, s], h_hi[:, i, :], start=i == 0, stop=False)
                        mm(o, wh[:, i, s], h_lo[:, i, :], start=False, stop=False)
                        ins = mm(o, wl[:, i, s], h_hi[:, i, :], start=False, stop=i == KT - 1)
                done(name, ins)

            pe.wait_ge(signal("h_split"), 1)
            for j in range(4):
                for b, y in enumerate((zg, zd, zx)):
                    split_channels(f"sg{b}{j}")
                    if j == 0:
                        pe.wait_ge(*read(("yt3", "do3", "xo3")[b]))
                    project_channels(f"bo{b}{j}", y)
            pe.wait_ge(signal("merged1"), 4)
            for j in range(4):
                project_tokens(f"wo{j}", merged)

            transpose_tokens("y", xn)
            pe.wait_ge(*read("Ty3"))
            w = unit_here("beta")
            bank = open_bank("ba")
            for q in range(2):
                for i in range(KT):
                    ins = mm(bank[0:4, 256 * q:256 * q + 256], w[:, i, 4 * q:4 * q + 4], hT[:, i, :],
                             start=i == 0, stop=i == KT - 1)
            done("ba", ins)
            bank = open_bank("gates")
            for t in range(TT):
                for i in range(KT):
                    ins = mm(bank[:, 24 * t:24 * t + 24], hT[:, i, 128 * t:128 * t + 128], w[:, i, 8:32],
                             start=i == 0, stop=i == KT - 1)
            done("gates", ins)
            freed_by["beta"] = "gates"
            for j in range(6):
                project_channels(f"c{j}", hT)
            project_channels("kcks", hT)
            project_channels("kwvc", hT)
            project_tokens("vsvw", hT)
            project_channels("nq0", hT)
            project_channels("nq1", hT)

            def rope_turn(name, a, n):
                bank = open_bank(name)
                done(name, mm(bank[:, 0:256 * n], const("rope"), ns[:, a:a + n, :], start=True, stop=True))

            pe.wait_ge(*read("nq1"))
            pe.wait_ge(*read("kwvc"))
            rope_turn("r0", 0, 2)
            rope_turn("r1", 2, 1)
            rope_turn("r2", 4, 2)
            rope_turn("r3", 6, 2)
            project_channels("z0", hT)
            project_channels("z1", hT)
            for kv, tile, ready in ((0, 0, "rope_done"), (1, 3, "rope_done")):
                pe.wait_ge(signal(ready), 4)
                bank = open_bank(f"sh{kv}")
                for g in range(2):
                    ins = mm(bank[:, 256 * g:256 * g + 256], const("selg")[:, 128 * g:128 * g + 128],
                             ns[:, tile, :], start=True, stop=True)
                done(f"sh{kv}", ins)
            pe.wait_ge(signal("squares"), 4)
            bank = open_bank("ss")
            for t in range(TT):
                for i in range(8):
                    ins = mm(bank[:, 8 * t + i:8 * t + i + 1], sq[:, i, 128 * t:128 * t + 128], const("ones"),
                             start=True, stop=True)
            done("ss", ins)
            pe.wait_ge(signal("row_gc"), 1)
            for j in range(2):
                bank = open_bank(f"gb{j}")
                for hh in range(2):
                    ins = mm(bank[:, 256 * hh:256 * hh + 256], rowsel[0:4, 2 * j + hh, :], row_gc, start=True, stop=True)
                done(f"gb{j}", ins)
            pe.wait_ge(signal("row_exp"), 2)
            pe.wait_ge(signal("row_g"), 1)
            bank = open_bank("cols")
            for t in range(TT):
                for q, row in enumerate((row_beta, row_g, row_last, row_gc)):
                    at = 16 * t + 4 * q
                    ins = nc.tensor.transpose(bank[:, at:at + 4], row[:, 128 * t:128 * t + 128], ident[0:4, 0:4])
            done("cols", ins)
            pe.wait_ge(signal("norm_cols"), 1)
            bank = open_bank("nr")
            for t in range(TT):
                ins = nc.tensor.transpose(bank[0:8, 128 * t:128 * t + 128], norm_cols[:, 8 * t:8 * t + 8], ident)
            done("nr", ins)
            pe.wait_ge(*read("nr"))
            for j in range(4):
                bank = open_bank(f"rb{j}")
                for hh in range(2):
                    ins = mm(bank[:, 256 * hh:256 * hh + 256], rowsel[0:8, 2 * j + hh, :], norm_rows, start=True, stop=True)
                done(f"rb{j}", ins)
            w = (unit_here("w1k", 16), unit_here("w1v", 16))
            bank = open_bank("hid")
            for kv in range(2):
                pe.wait_ge(*read(f"sh{kv}"))
                for j in range(16):
                    ins = mm(bank[:, 32 * kv:32 * kv + 30], w[kv][:, j, :], cblk[kv][:, j, :], start=j == 0, stop=j == 15)
            done("hid", ins)
            freed_by["w1k"] = freed_by["w1v"] = "hid"

            pe.wait_ge(*read("rb3"))
            for t in range(TT):
                bank = open_bank(f"kk{t}")
                for h in range(4):
                    ins = nc.tensor.transpose(bank[:, 128 * h:128 * h + 128], cv[:, 4 + h, 128 * t:128 * t + 128], ident)
                done(f"kk{t}", ins)
            for t in range(TT):
                bank = open_bank(f"vt{t}")
                for h in range(4):
                    ins = nc.tensor.transpose(bank[:, 128 * h:128 * h + 128], cv[:, 8 + h, 128 * t:128 * t + 128], ident)
                done(f"vt{t}", ins)
            for name, a in (("kg", 4), ("qg", 0)):
                for t in range(TT):
                    bank = open_bank(f"{name}{t}")
                    for h in range(4):
                        ins = mm(bank[:, 128 * h:128 * h + 128], cv[:, 4 + h, 128 * t:128 * t + 128],
                                 cv[:, a + h, 128 * t:128 * t + 128], start=True, stop=True)
                    done(f"{name}{t}", ins)
            pe.wait_ge(*read("hid"))
            pe.wait_ge(signal("w2_in"), 32)
            bank = open_bank("kcv")
            for g in range(2):
                mm(bank[64 * g:64 * g + 64, 0:15], w2k, hid[:, 15 * g:15 * g + 15], start=True, stop=True)
            for g in range(2):
                ins = mm(bank[0:15, 64 + 64 * g:128 + 64 * g], hid[:, 32 + 15 * g:47 + 15 * g], w2v, start=True, stop=True)
            done("kcv", ins)
            pe.wait_ge(*read("kcv"))
            for g in range(2):
                bank = open_bank(f"cs{g}")
                for t in range(TT):
                    for r in range(4):
                        at = 64 * t + 16 * r
                        ins = mm(bank[:, at:at + 15], ns[64 * g:64 * g + 64, 4 + r, 128 * t:128 * t + 128],
                                 kcT[64 * g:64 * g + 64, 0:15], start=True, stop=True)
                done(f"cs{g}", ins)

            pe.wait_ge(signal("level_mask"), 1)
            for t in range(TT):
                bank = open_bank(f"t0{t}")
                for h in range(4):
                    ins = nc.tensor.transpose(bank[:, 128 * h:128 * h + 128], nAm[0][:, 4 * t + h, :], ident)
                done(f"t0{t}", ins)

            def level(n):
                pe.wait_ge(signal("level_mask"), n + 1)
                for t in range(TT):
                    pe.wait_ge(*read(f"{'t0' if n == 1 else 'xt' + str(n - 1)}{t}"))
                    bank = open_bank(f"lz{n}{t}")
                    for h in range(4):
                        ins = mm(bank[:, 128 * h:128 * h + 128], nAm[n % 2][:, 4 * t + h, :], TmT[:, 4 * t + h, :],
                                 start=True, stop=True)
                    done(f"lz{n}{t}", ins)

            def level_end(n):
                for t in range(TT):
                    pe.wait_ge(*read(f"lz{n}{t}"))
                    if n < 5:
                        bank = open_bank(f"xx{n}{t}")
                        for h in range(4):
                            ins = mm(bank[:, 128 * h:128 * h + 128], zst[:, 4 * t + h, :], Tm[:, 4 * t + h, :],
                                     start=True, stop=True)
                        done(f"xx{n}{t}", ins)
                    bank = open_bank(f"xt{n}{t}")
                    for h in range(4):
                        ins = mm(bank[:, 128 * h:128 * h + 128], Tm[:, 4 * t + h, :], zst[:, 4 * t + h, :],
                                 start=True, stop=True)
                    done(f"xt{n}{t}", ins)

            def nsa_logits(i):
                h, b = i // 2, i % 2
                r, g = h // 2, h % 2
                causal_logits(f"nl{i}", ns[:, 4 + r, :], ns[:, 1 + b, :], (64 * g, 64 * g + 64))

            def nsa_transposes(i):
                pe.wait_ge(signal("nprob"), i + 1)
                causal_transposes(f"np{i}", i % 3)

            def nsa_out(r):
                bank = open_bank(f"no{r}")
                for g in range(2):
                    o = bank[64 * g:64 * g + 64, 0:256]
                    for b in range(2):
                        i = 2 * (2 * r + g) + b
                        v0 = 128 * b + 64 * g
                        pT = nprobT[i % 4]
                        pe.wait_ge(*read(f"np{i}"))
                        mm(o, v_tok[:, 0, v0:v0 + 64], pT[:, 0:256], start=b == 0, stop=False, skip_group_check=True)
                        mm(o[:, 128:256], v_tok[:, 1, v0:v0 + 64], pT[:, 256:384], start=False, stop=False,
                           skip_group_check=True)
                    ins = mm(o, vcn[0:15, 64 * g:64 * g + 64], pcT[0:15, 256 * (4 * g + r):256 * (4 * g + r) + 256],
                             start=False, stop=True, skip_group_check=True)
                done(f"no{r}", ins)

            level(1)
            project_channels("ma0", hT)
            level_end(1)
            pe.wait_ge(signal("cprob"), 1)
            for j in range(4):
                bank = open_bank(f"cp{j}")
                for hh in range(2):
                    for t in range(TT):
                        ins = nc.tensor.transpose(bank[0:15, 256 * hh + 128 * t:256 * hh + 128 * t + 128],
                                                  pc[:, t, 16 * (2 * j + hh):16 * (2 * j + hh) + 15], ident)
                done(f"cp{j}", ins)
            project_channels("ma1", hT)
            level(2)
            project_channels("ma2", hT)
            level_end(2)
            project_channels("ma3", hT)
            level(3)
            project_channels("mb0", hT)
            level_end(3)
            project_channels("mb1", hT)
            level(4)
            project_channels("mb2", hT)
            level_end(4)
            project_channels("mb3", hT)
            level(5)
            nsa_logits(0)
            nsa_logits(1)
            level_end(5)
            for t in range(TT):
                pe.wait_ge(*read(f"xt5{t}"))
                bank = open_bank(f"u{t}")
                for h in range(4):
                    ins = mm(bank[:, 128 * h:128 * h + 128], TmT[:, 4 * t + h, :], vb[:, 4 * t + h, :], start=True, stop=True)
                done(f"u{t}", ins)
                bank = open_bank(f"wt{t}")
                for h in range(4):
                    ins = mm(bank[:, 128 * h:128 * h + 128], kbe[:, 4 * t + h, :], TmT[:, 4 * t + h, :], start=True, stop=True)
                done(f"wt{t}", ins)

            def gdn_chunk(c):
                t, r = c // 2, 64 * (c % 2)
                if c > 0:
                    pe.wait_ge(*read(f"gs{c - 1}"))
                    pe.wait_ge(*read("wt1"))
                    bank = open_bank(f"ws{c}")
                    for h in range(4):
                        ins = mm(bank[r:r + 64, 128 * h:128 * h + 128], wT[:, 4 * t + h, r:r + 64],
                                 gstate[c - 1][:, 128 * h:128 * h + 128], start=True, stop=True)
                    done(f"ws{c}", ins)

            def gdn_state(c):
                t, r = c // 2, 64 * (c % 2)
                pe.wait_ge(*((signal("v_new"), 1) if c == 0 else read(f"ws{c}")))
                bank = open_bank(f"gs{c}")
                for h in range(4):
                    ins = mm(bank[:, 128 * h:128 * h + 128], kdt[r:r + 64, 4 * t + h, :], v_new[r:r + 64, 4 * t + h, :],
                             start=True, stop=True)
                done(f"gs{c}", ins)

            def nsa_step(i):
                if i + 2 < 16:
                    nsa_logits(i + 2)
                nsa_transposes(i)
                if i % 4 == 3:
                    nsa_out(i // 4)

            nsa_step(0)
            gdn_state(0)
            nsa_step(1)
            gdn_chunk(1)
            nsa_step(2)
            gdn_state(1)
            nsa_step(3)
            gdn_chunk(2)
            nsa_step(4)
            gdn_state(2)
            nsa_step(5)
            gdn_chunk(3)
            nsa_step(6)
            pe.wait_ge(*read("ws3"))
            pe.wait_ge(signal("qk_masked"), 1)
            pe.wait_ge(signal("q_decayed"), 1)
            for t in range(TT):
                bank = open_bank(f"gd{t}")
                for h in range(4):
                    o = bank[:, 128 * h:128 * h + 128]
                    mm(o, qkT[:, 4 * t + h, :], v_new[:, 4 * t + h, :], start=True, stop=True)
                    for c in (2 * t, 2 * t + 1):
                        if c > 0:
                            r = 64 * (c % 2)
                            ins = mm(o[r:r + 64, :], egc[:, h, 64 * c:64 * c + 64],
                                     gstate[c - 1][:, 128 * h:128 * h + 128], start=False, stop=True,
                                     skip_group_check=True)
                done(f"gd{t}", ins)
            for i in range(7, 16):
                nsa_step(i)
            pe.wait_ge(*read("gd1"))
            for j in range(2):
                bank = open_bank(f"gt{j}")
                for hh in range(2):
                    for t in range(TT):
                        ins = nc.tensor.transpose(bank[:, 256 * hh + 128 * t:256 * hh + 128 * t + 128],
                                                  nA[:, 4 * t + 2 * j + hh, :], ident)
                done(f"gt{j}", ins)
            pe.wait_ge(*read("no3"))
            pe.wait_ge(*read("gt1"))
            for j in range(2):
                project_channels(f"bg{j}", z2, k=4, width=512)
                project_channels(f"bn{j}", oT, k=4, width=512)
            pe.wait_ge(signal("merged2"), 4)
            for j in range(4):
                project_tokens(f"w2o{j}", ma)
            transpose_tokens("f", xn)
            pe.wait_ge(*read("Tf3"))
            for j in range(FT):
                split_channels(f"gu{j}")
            for c in range(4):
                bank = open_bank(f"wd{c}")
                for q, k0 in enumerate(range(0, FT, 8)):
                    if c == 0:
                        pe.wait_ge(*read(f"gu{min(k0 + 8, FT) - 1}"))
                    wh, wl = unit_here(f"wd{c}{q}")
                    for t in range(TT):
                        o = bank[:, 256 * t:256 * t + 256]
                        for i in range(k0, min(k0 + 8, FT)):
                            fh, fl = (f[:, i, 128 * t:128 * t + 128] for f in (f_hi, f_lo))
                            mm(o, fh, wh[:, i - k0, :], start=i == 0 and t == 0, stop=False, skip_group_check=True)
                            mm(o, fh, wl[:, i - k0, :], start=False, stop=False, skip_group_check=True)
                            ins = mm(o, fl, wh[:, i - k0, :], start=False, stop=i == FT - 1, skip_group_check=True)
                    if q < 2:
                        ins.then_inc(signal("down_part"), 1)
                done(f"wd{c}", ins)

        @block.sync
        def _(sp):
            sp.dma_start(xres, A["x"][0].rearrange("(t p) d -> p t d", p=128)).then_inc(signal("x_in"), 16)
            sp.dma_start(flat(cst_at, NCONST), consts).then_inc(signal("consts"), 16)
            sp.wait_ge(signal("params"), 16 * 14)
            for i, name in enumerate(order):
                s = i % NSLOT
                if i >= NSLOT:
                    freed = freed_by[order[i - NSLOT]]
                    if isinstance(freed, tuple):
                        sp.wait_ge(signal(freed[0]), freed[1])
                    else:
                        sp.wait_ge(*full(freed))
                pieces, width = units[name]
                if name in ("w1k", "w1v"):
                    v = pieces.rearrange("(j q) d h -> q d j h", q=2)
                    for q in range(2):
                        sp.dma_start(ring[64 * q:64 * q + 64, s, :].rearrange("p (j h) -> p j h", j=16), v[q])\
                          .then_inc(slot_loaded[s], 16)
                elif name.startswith("bn"):
                    for g in range(2):
                        v = pieces[256 * g:256 * g + 256, :].rearrange("(r d) c -> d r c", d=64)
                        sp.dma_start(ring[64 * g:64 * g + 64, s, :].rearrange("p (k c) -> p k c", k=4),
                                     v[:, :, width:width + 512]).then_inc(slot_loaded[s], 16)
                else:
                    dst = ring[:, s, :].rearrange("p (k c) -> p k c", c=width)
                    for src, k, at in pieces:
                        sp.dma_start(dst[:, 0:k, at:at + src.shape[2]], src).then_inc(slot_loaded[s], 16)
                if name == "iq1":
                    sp.wait_ge(*read("tb7"))
                    sp.dma_start(bias_rows.rearrange("h p m -> p h m"), bias_out).then_inc(signal("bias_rows_out"), 16)
                if name == "zd3":
                    sp.wait_ge(*full("og3"))
                    sp.wait_ge(*full("kt1"))
                    sp.wait_ge(signal("bias_rows_out"), 16)
                    for h in range(DH):
                        v = bass.AP(bias_rows.tensor, h * 128 * 383 + 127, [[382, 128], [1, 256]])
                        sp.dma_start(toep[:, h, :], v).then_inc(signal("toep_in"), 16)
                if name == "sg13":
                    sp.dma_start(g_post, A["g_post"].broadcast_to([128, D])).then_inc(signal("g_post_in"), 16)
                if name == "gu3":
                    sp.dma_start(g_fin, A["final_norm_gain_2"].rearrange("(a n) -> a n", a=1).broadcast_to([128, D]))\
                      .then_inc(signal("g_fin_in"), 16)
            sp.wait_ge(signal("result"), 1)
            sp.dma_start(out[0].rearrange("(t p) d -> p t d", p=128), xn).then_inc(signal("out_done"), 16)
            sp.wait_ge(signal("out_done"), 16)

        def stepper(eng, name):
            count = [0]

            def step(ins):
                count[0] += 1
                ins.then_inc(signal(name), 1)
                eng.wait_ge(signal(name), count[0])
            return step

        tanh_users = [f"zx{j}" for j in range(4)] + [f"zg{j}" for j in range(4)] + [f"zd{j}" for j in range(4)]
        tanh_users += [f"bo{b}{j}" for j in range(4) for b in range(3)]
        tanh_users += [f"conv{j}" for j in range(6)] + ["z0", "z1"] + [f"gu{j}" for j in range(FT)]

        def tanh_read(name):
            if name.startswith("conv"):
                return signal("silu_done"), int(name[4:]) + 1
            return read(name)

        @block.scalar
        def _(sc):
            step = stepper(sc, "act_step")
            at = 0
            for name in ("g_pre", "g_mem", "mix_norm_gain_2", "ffn_norm_gain_2", "g_gla", "b_gla_a",
                         "gdn_conv_w_2", "gdn_out_norm_gain_2", "cmp_pos_k_2", "cmp_pos_v_2"):
                v = A[name][0]
                if name == "gdn_conv_w_2":
                    v = v.rearrange("j (k p) -> (j k) p", p=128)
                elif name.startswith("cmp"):
                    v = v.rearrange("(j q) d -> j (q d)", q=2)
                else:
                    v = v.rearrange("(k p) -> k p", p=128)
                sc.dma_start(par_rows[at:at + v.shape[0], :], v).then_inc(signal("params"), 16)
                at += v.shape[0]
            assert at == 119
            for dst, src in ((rel, A["rel_bias"]), (w_up, A["w_gla_a_up"][0]),
                             (a_log, A["gdn_a_log_2"][0].rearrange("(h a) -> h a", a=1)),
                             (dt_bias, A["gdn_dt_bias_2"][0].rearrange("(h a) -> h a", a=1))):
                sc.dma_start(dst, src).then_inc(signal("params"), 16)

            def squares(tag, src, col, wait):
                sc.wait_ge(*wait)
                for t in range(TT):
                    ins = act(probT[:, 0:2, :].rearrange("p a b -> p (a b)"), src[:, t, :], ACT.Square,
                              accum_out=sumsq[:, col + t:col + t + 1])
                    if t == 0:
                        step(ins)
                ins.then_inc(signal(f"sumsq_{tag}"), 1)
                sc.wait_ge(signal(f"sumsq_{tag}"), 1)

            def copy(name, dst, src=None, scale=None):
                sc.wait_ge(*full(name))
                src = bank_of(name)[:, :] if src is None else src
                act(dst, src, ACT.Copy, scale=1.0 if scale is None else scale).then_inc(bank_read[turns[name] % 8], 1)

            def pair(tiles_, j):
                return tiles_[:, 2 * j:2 * j + 2, :].rearrange("p a b -> p (a b)")

            def copy_tokens(name, dst, c):
                copy(name, dst[:, :, 256 * c:256 * c + 256], bank_of(name)[:, :].rearrange("p (t c) -> p t c", t=TT))

            def tanh(user, src, wait, inc=None, n=512):
                i = tanh_users.index(user)
                if i >= 2:
                    sc.wait_ge(*tanh_read(tanh_users[i - 2]))
                sc.wait_ge(*wait)
                act(tnh[:, i % 2, 0:n], src, ACT.Tanh, scale=0.5).then_inc(inc or signal("tanh_done"), 1)

            squares("x", xres, 0, (signal("x_in"), 16))
            squares("m", memn, 2, (signal("mem_in"), 16))
            for h in range(DH):
                copy(f"tb{h}", bias_out[:, h, :], bank_of(f"tb{h}")[:, 0:383])
            sc.wait_ge(*full("ikga"))
            act(ikT, bank_of("ikga")[:, 0:256], ACT.Copy)
            act(gaT, bank_of("ikga")[0:RANK, 256:512], ACT.Copy).then_inc(bank_read[turns["ikga"] % 8], 1)
            for j in range(2):
                copy(f"iq{j}", pair(iq, j))
            for i, name in enumerate(("is00", "is01", "is10", "is11", "is12", "is13")):
                sc.wait_ge(*full(name))
                if i >= 2:
                    sc.wait_ge(signal("relu_used"), i - 1)
                act(relu[:, i % 2, :], bank_of(name)[:, :], ACT.Relu).then_inc(bank_read[turns[name] % 8], 1)
            for j in range(4):
                copy(f"mk{j}", pair(mk, j))
            sc.wait_ge(*full("Tm3"))
            for j in range(4):
                copy_tokens(f"mv{j}", mv, j)
            for j in range(4):
                copy(f"xq{j}", pair(xq, j))
            for j in range(4):
                tanh(f"zx{j}", bank_of(f"zx{j}")[:, :], full(f"zx{j}"))

            def cross_exp(h):
                sc.wait_ge(signal("xmax"), h + 1)
                if h == 3:
                    sc.wait_ge(*full("xp0"))
                for t in range(TT):
                    ins = act(prob[:, h % 3, 256 * t:256 * t + 256], bank_of(f"xl{h}")[:, 256 * t:256 * t + 256],
                              ACT.Exp, bias=neg_max[:, 2 * h + t:2 * h + t + 1], scale=256 ** -0.5,
                              accum_out=p_sum[:, 2 * h + t:2 * h + t + 1])
                ins.then_inc(bank_read[turns[f"xl{h}"] % 8], 1)

            def cross_copy(h):
                if h == 3:
                    sc.wait_ge(*full("xo0"))
                copy(f"xp{h}", probT[:, h % 3, :])

            cross_exp(0)
            cross_exp(1)
            copy("gq0", pair(gq, 0))
            cross_exp(2)
            copy("gq1", pair(gq, 1))
            cross_copy(0)
            cross_exp(3)
            copy("gk0", pair(gk, 0))
            cross_copy(1)
            copy("gk1", pair(gk, 1))
            sc.wait_ge(*full("xl3"))
            for j in range(2):
                sc.wait_ge(*full(f"ax{j}"))
                for hh in range(2):
                    h = 2 * j + hh
                    ins = act(expo[:, h, :], bank_of(f"ax{j}")[:, 256 * hh:256 * hh + 256], ACT.Abs, bias=b_gla[:, h:h + 1])
                ins.then_inc(signal("gate_abs"), 1)
            sc.wait_ge(signal("gate_abs"), 2)
            step(act(expo, expo, ACT.Exp, scale=-1.0))
            act(expo, expo, ACT.Ln, bias=1.0).then_inc(signal("gate_ln"), 1)
            cross_copy(2)
            copy_tokens("gv0", gv, 0)
            cross_copy(3)
            copy_tokens("gv1", gv, 1)
            copy_tokens("gv2", gv, 2)
            copy_tokens("gv3", gv, 3)
            copy("dk0", pair(dk, 0))
            copy_tokens("dv0", dv, 0)
            sc.wait_ge(signal("gate_cum"), 1)
            act(cumlog, expo, ACT.Exp, scale=1 / 16).then_inc(signal("gate_exp"), 1)
            act(k_d, expo, ACT.Exp, scale=-1 / 16).then_inc(signal("gate_exp"), 1)
            act(decay1.rearrange("p (h c) -> p h c", h=4),
                expo.rearrange("p h (c t) -> p h c t", t=CH)[:, :, :, CH - 1], ACT.Exp, scale=1 / 16)
            sc.wait_ge(signal("gate_diff"), 1)
            act(expo_last, expo_last, ACT.Exp, scale=1 / 16).then_inc(signal("gate_exp"), 1)
            for j in range(4):
                copy(f"dq{j}", pair(dq, j))
            for j in range(TT):
                copy(f"kt{j}", kt_tok[:, 4 * j:4 * j + 4, :].rearrange("p a b -> p (a b)"))
            sc.wait_ge(signal("bias_rows_out"), 16)
            for j in range(4):
                tanh(f"zg{j}", bank_of(f"zg{j}")[:, :], full(f"zg{j}"))
            for h in range(H1):
                sc.wait_ge(*full(f"og{h}"))
                for t in range(TT):
                    ins = act(probT[:, 2, 0:256], bank_of(f"og{h}")[:, 256 * t:256 * t + 256], ACT.Square,
                              accum_out=sumsq[:, 8 + 2 * h + t:9 + 2 * h + t])
                    if t == 0:
                        step(ins)
                ins.then_inc(signal("sumsq_g"), 1)
                sc.wait_ge(signal("sumsq_g"), h + 1)
            for j in range(4):
                tanh(f"zd{j}", bank_of(f"zd{j}")[:, :], full(f"zd{j}"))

            def causal_exp(pre, i):
                sc.wait_ge(signal(pre + "max"), i + 1)
                for t, (a, b) in enumerate(((0, 128), (128, 384))):
                    c = 2 * (i % 8) + t
                    ins = act(prob[:, i % 3, a:b], prob[:, i % 3, a:b], ACT.Exp, bias=neg_max[:, c:c + 1],
                              accum_out=p_sum[:, c:c + 1])
                ins.then_inc(signal(pre + "exp"), 1)

            for h in range(DH + 2):
                if h < DH:
                    causal_exp("d", h)
                if h >= 2:
                    i = h - 2
                    if i >= 3:
                        sc.wait_ge(*full(f"do{(i - 3) // 2}"))
                    copy(f"dp{i}", probT[:, i % 3, 0:384], bank_of(f"dp{i}")[:, 0:384])
            def high_part(n):
                name = split_units[n]
                m = 256 * ffn_tiles(name)
                sc.wait_ge(*loaded[name])
                if n not in (0, 1, nsg, nsg + 1):
                    sc.wait_ge(*ffn_free(n - 2))
                act(w_hi[:, n % 2, 0:m], ring[:, order.index(name) % NSLOT, 0:m], ACT.Copy).then_inc(signal("w_high"), 1)

            sc.wait_ge(signal("bias_pen"), DH)
            act(h_hi[:, :, :], hT, ACT.Copy).then_inc(signal("h1_high"), 1)
            high_part(0)
            high_part(1)
            for j in range(4):
                for b in range(3):
                    if 3 * j + b + 2 < nsg:
                        high_part(3 * j + b + 2)
                    tanh(f"bo{b}{j}", bank_of(f"sg{b}{j}")[:, :], full(f"sg{b}{j}"),
                         inc=bank_read[turns[f"sg{b}{j}"] % 8])
            for j in range(4):
                copy_tokens(f"wo{j}", xn, j)
            squares("wo", xn, 4, read("wo3"))

            squares("y", xres, 0, (signal("x_mid"), 1))
            step(act(a_pos, a_log, ACT.Exp))
            sc.wait_ge(*full("ba"))
            act(row_beta, bank_of("ba")[0:4, 0:256], ACT.Tanh, scale=0.5).then_inc(signal("beta_tanh"), 1)
            sc.wait_ge(*read("ba"))
            step(act(row_b, row_a, ACT.Abs))
            step(act(row_b, row_b, ACT.Exp, scale=-1.0))
            act(row_b, row_b, ACT.Ln, bias=1.0).then_inc(signal("alpha_ln"), 1)
            sc.wait_ge(*full("gates"))
            act(gate_tok.rearrange("p a b -> p (a b)"), bank_of("gates")[:, 0:48], ACT.Tanh, scale=0.5)\
                .then_inc(bank_read[turns["gates"] % 8], 1)
            sc.wait_ge(signal("row_gc"), 1)
            sc.wait_ge(signal("row_diff"), 1)
            act(row_b, row_gc, ACT.Exp).then_inc(signal("row_exp"), 1)
            act(row_last, row_last, ACT.Exp).then_inc(signal("row_exp"), 1)

            def conv_tanh(j):
                tanh(f"conv{j}", pair(cv, j), (signal("conv_done"), j + 1))

            for j in range(6):
                copy(f"c{j}", raw[:, 2 * j:2 * j + 2, 3:S + 3], bank_of(f"c{j}")[:, :].rearrange("p (a b) -> p a b", a=2))
                if j >= 1:
                    conv_tanh(j - 1)
            copy("kcks", pair(ns, 0))
            copy("kwvc", pair(ns, 1))
            copy_tokens("vsvw", v_tok, 0)
            copy("nq0", pair(ns, 2))
            copy("nq1", pair(ns, 3))
            conv_tanh(5)
            sc.wait_ge(signal("silu_done"), 6)
            for j in range(4):
                act(pair(sq, j), pair(cv, j), ACT.Square, scale=0.5).then_inc(signal("squares"), 1)
            for j in range(2):
                tanh(f"z{j}", bank_of(f"z{j}")[:, :], full(f"z{j}"))
            for j in range(2):
                sc.wait_ge(*full(f"gb{j}"))
                act(pair(egc, j), bank_of(f"gb{j}")[:, :], ACT.Exp).then_inc(signal("egc"), 1)
            copy("cols", cols[:, :, 0:16], bank_of("cols")[:, 0:32].rearrange("p (t c) -> p t c", t=TT))
            sc.wait_ge(*full("hid"))
            hb = bank_of("hid")[:, 0:64].rearrange("p (a b) -> p a b", a=2)[:, :, 0:30]
            act(pc[:, :, 0:30], hb, ACT.Tanh, scale=0.5).then_inc(signal("hid_tanh"), 1)
            sc.wait_ge(signal("d_min"), 1)
            act(qkT, qkT, ACT.Exp).then_inc(signal("d_exp"), 1)
            act(nA, nA, ACT.Exp, scale=-1.0).then_inc(signal("d_exp"), 1)
            sc.wait_ge(*full("kcv"))
            act(kcT[:, 0:15], bank_of("kcv")[:, 0:15], ACT.Copy, scale=0.5)
            act(vcn[0:15, :], bank_of("kcv")[0:15, 64:192], ACT.Copy, scale=0.5).then_inc(bank_read[turns["kcv"] % 8], 1)
            sc.wait_ge(signal("cmax"), 1)
            pcv = pc.rearrange("p t (h n) -> p (t h) n", n=16)[:, :, 0:15]
            act(pcv, pcv, ACT.Exp).then_inc(signal("cexp"), 1)

            def level_copy(n):
                for t in range(TT):
                    copy(f"lz{n}{t}", zst[:, 4 * t:4 * t + 4, :].rearrange("p a b -> p (a b)"))

            def merge_gate(name):
                dst, j = (ma, mb)[name[1] == "b"], int(name[2])
                sc.wait_ge(*full(name))
                act(pair(dst, j), bank_of(name)[:, :], ACT.Tanh, scale=0.5).then_inc(bank_read[turns[name] % 8], 1)

            def nsa_copy(i):
                if i >= 4:
                    sc.wait_ge(*full(f"no{(i - 4) // 4}"))
                copy(f"np{i}", nprobT[i % 4], bank_of(f"np{i}")[:, 0:384])

            level_copy(1)
            merge_gate("ma0")
            for j in range(4):
                copy(f"cp{j}", pcT[0:15, 512 * j:512 * j + 512], bank_of(f"cp{j}")[0:15, :])
            merge_gate("ma1")
            level_copy(2)
            merge_gate("ma2")
            merge_gate("ma3")
            level_copy(3)
            merge_gate("mb0")
            merge_gate("mb1")
            level_copy(4)
            merge_gate("mb2")
            merge_gate("mb3")
            level_copy(5)
            causal_exp("n", 0)
            causal_exp("n", 1)
            for t in range(TT):
                if t == 0:
                    sc.wait_ge(*full("xt51"))
                copy(f"u{t}", u_tok[:, 4 * t:4 * t + 4, :].rearrange("p a b -> p (a b)"))
                copy(f"wt{t}", wT[:, 4 * t:4 * t + 4, :].rearrange("p a b -> p (a b)"))
            for i in range(16):
                if i + 2 < 16:
                    causal_exp("n", i + 2)
                nsa_copy(i)
                if i % 4 == 3:
                    copy(f"no{i // 4}", oT[:, i // 4, :], bank_of(f"no{i // 4}")[:, 0:256])
                if i == 6:
                    for t in range(TT):
                        sc.wait_ge(*full(f"gd{t}"))
                        for h in range(4):
                            ins = act(tnh[:, 0, 0:128], bank_of(f"gd{t}")[:, 128 * h:128 * h + 128], ACT.Square,
                                      accum_out=sumsq[:, 8 + 4 * t + h:9 + 4 * t + h])
                            if 4 * t + h < 7:
                                step(ins)
                    ins.then_inc(signal("sumsq_d"), 1)
            squares("f", xres, 4, read("w2o3"))

            high_part(nsg)
            high_part(nsg + 1)
            for n in range(2, len(ffn_units)):
                high_part(nsg + n)
                if n - 2 < FT:
                    tanh(f"gu{n - 2}", bank_of(f"gu{n - 2}")[:, 0:256], full(f"gu{n - 2}"), n=256)
            squares("o", xres, 6, read("wd3"))

        @block.gpsimd
        def _(gp):
            step = stepper(gp, "pool_step")
            gp.dma_start(memn, A["mem"][0].rearrange("(t p) d -> p t d", p=128)).then_inc(signal("mem_in"), 16)
            gp.memset(attT, 0.0).then_inc(signal("att_zero"), 1)
            gp.wait_ge(signal("consts"), 16)

            def rsqrt_mean(tag, col, n, width, count=1):
                gp.wait_ge(signal(f"sumsq_{tag}"), count)
                step(nc.gpsimd.tensor_scalar(var[:, col:col + n], sumsq[:, col:col + n], 1 / width, EPS, ALU.mult, ALU.add))
                nc.gpsimd.tensor_tensor(rstd[:, col:col + n], var[:, col:col + n], mhalf.broadcast_to([128, n]), ALU.pow)\
                    .then_inc(signal(f"rstd_{tag}"), 1)

            rsqrt_mean("x", 0, 2, D)
            rsqrt_mean("m", 2, 2, D)
            for h in range(H1):
                rsqrt_mean("g", 8 + 2 * h, 2, DV, h + 1)

            def bias_and_pen(h):
                if h == 0:
                    gp.wait_ge(signal("toep_in"), 16 * DH)
                    gp.wait_ge(signal("pen_ready"), 1)
                if h >= 2:
                    gp.wait_ge(*read(f"dl{h - 2}"))
                nc.gpsimd.tensor_tensor(bias_pen[:, h % 2, 0:128], toep[:, h, 128:256], pen[:, 0:128], ALU.add)
                nc.gpsimd.tensor_tensor(bias_pen[:, h % 2, 128:384], toep[:, h, :], pen[:, 128:384], ALU.add)\
                    .then_inc(signal("bias_pen"), 1)

            for h in range(DH):
                bias_and_pen(h)
            rsqrt_mean("wo", 4, 2, D)
            rsqrt_mean("y", 0, 2, D)
            gp.dma_start(w2k, A["cmp_w2_k_2"][0]).then_inc(signal("w2_in"), 16)
            gp.dma_start(w2v, A["cmp_w2_v_2"][0]).then_inc(signal("w2_in"), 16)
            nc.gpsimd.memset(raw[:, :, 0:3], 0.0).then_inc(signal("conv_pad"), 1)
            for i, (name, a, n) in enumerate((("r0", 0, 2), ("r1", 2, 1), ("r2", 4, 2), ("r3", 6, 2))):
                gp.wait_ge(*full(name))
                cosb = const("cos").unsqueeze(1).broadcast_to([128, n, S])
                nc.gpsimd.tensor_tensor(ns[:, a:a + n, :], ns[:, a:a + n, :], cosb, ALU.mult).then_inc(signal("rope_cos"), 1)
            gp.wait_ge(*read("ss"))
            nc.gpsimd.tensor_tensor(norm_cols, norm_cols, mhalf.broadcast_to([128, 16]), ALU.pow)\
                .then_inc(signal("norm_cols"), 1)
            gp.wait_ge(*read("rb1"))
            gp.wait_ge(signal("decay2"), 1)
            nc.gpsimd.tensor_tensor(egc, egc, cv[:, 0:4, :], ALU.mult).then_inc(signal("q_decayed"), 1)

            def level_mask(n):
                if n >= 2:
                    gp.wait_ge(*full(f"lz{n - 2}1" if n > 2 else "t01"))
                    gp.wait_ge(signal("T_start"), 1)
                m = const("lev")[:, 128 * n:128 * n + 128].unsqueeze(1).broadcast_to([128, 8, 128])
                nc.gpsimd.tensor_tensor(nAm[n % 2], nA, m, ALU.mult).then_inc(signal("level_mask"), 1)

            gp.wait_ge(signal("nA_ready"), 1)
            level_mask(0)
            level_mask(1)
            gp.wait_ge(*read("qg1"))
            m = const("chunk").unsqueeze(1).broadcast_to([128, 8, 128])
            nc.gpsimd.tensor_tensor(qkT, qkT, m, ALU.mult).then_inc(signal("qk_masked"), 1)
            for n in range(2, 6):
                level_mask(n)
            rsqrt_mean("d", 8, 8, 128)
            rsqrt_mean("f", 4, 2, D)
            rsqrt_mean("o", 6, 2, D)

        @block.vector
        def _(ve):
            step = stepper(ve, "dve_step")

            def pair(tiles_, j):
                return tiles_[:, 2 * j:2 * j + 2, :].rearrange("p a b -> p (a b)")

            def halves(name):
                return bank_of(name)[:, :].rearrange("p (t c) -> p t c", t=2)

            def reader(name):
                return bank_read[turns[name] % 8]

            def scale_rows(tag, dst, src, col):
                ve.wait_ge(signal(f"rstd_{tag}"), 1)
                for t in range(TT):
                    ins = tsc(dst[:, t, :], src[:, t, :], rstd[:, col + t:col + t + 1], None, ALU.mult)
                ins.then_inc(signal(f"scaled_{tag}"), 1)

            def transposed(tag, dst):
                for j in range(4):
                    ve.wait_ge(*full(f"T{tag}{j}"))
                    for kk in range(2):
                        k = 2 * j + kk
                        ins = tsc(dst[:, k, :], bank_of(f"T{tag}{j}")[:, 256 * kk:256 * kk + 256],
                                  gain[tag][:, k:k + 1], None, ALU.mult)
                    ins.then_inc(reader(f"T{tag}{j}"), 1)

            def twice_silu(name, dst):
                i = tanh_users.index(name)
                plain = [u for u in tanh_users[:i + 1] if not u.startswith("bo")]
                ve.wait_ge(signal("tanh_done"), len(plain))
                stt(dst, tnh[:, i % 2, :], 1.0, bank_of(name)[:, :], ALU.add, ALU.mult).then_inc(reader(name), 1)

            ve.wait_ge(signal("params"), 16 * 14)
            ve.wait_ge(*full("par"))
            nc.vector.tensor_copy(par[:, 0:119], bank_of("par")[:, 0:119]).then_inc(reader("par"), 1)
            ve.wait_ge(*read("par"))
            nc.vector.tensor_copy(relb, rel.unsqueeze(2).broadcast_to([32, DH, 128])).then_inc(signal("relb_ready"), 1)
            tsc(g_gla_half, g_gla, 0.5, None, ALU.mult)
            tsc(g_gdn_half, g_gdn, 0.5, None, ALU.mult)
            scale_rows("x", xn, xres, 0)
            scale_rows("m", memn, memn, 2)
            transposed("x", hT)
            ve.wait_ge(*full("iw"))
            tsc(iw.rearrange("p a b -> p (a b)"), bank_of("iw")[:, 0:16], IDX_H ** -0.5 * IDX_D ** -0.5, None, ALU.mult)\
                .then_inc(reader("iw"), 1)
            ve.wait_ge(*read("iw"))
            transposed("m", memT)
            for t in range(TT):
                n, per = (128, 4) if t == 0 else (256, 2)
                acc = score[:, 0:128] if t == 0 else score[:, 128:384]
                for j in range(IDX_H // per):
                    ve.wait_ge(*read(f"is{t}{j}"))
                    for hh, h in enumerate(index_heads(t, j)):
                        src = relu[:, j % 2, n * hh:n * hh + n]
                        if j == 0 and hh == 0:
                            ins = tsc(acc, src, iw[:, t, 0:1], None, ALU.mult)
                        else:
                            ins = stt(acc, src, iw[:, t, h:h + 1], acc, ALU.mult, ALU.add)
                        if hh < per - 1:
                            step(ins)
                    ins.then_inc(signal("relu_used"), 1)
                    ve.wait_ge(signal("relu_used"), j + 1 if t == 0 else j + 3)
            step(tt_(score, score, diag3, ALU.add))

            def top_keys(t):
                s = score[:, 0:128] if t == 0 else score[:, 128:384]
                for _ in range(TOPK // 8):
                    step(nc.vector.max(top8, s))
                    step(nc.vector.match_replace(s, top8, s, TAKEN))

            def cross_max(h):
                ve.wait_ge(*full(f"xl{h}"))
                step(nc.vector.reduce_max(neg_max[:, 2 * h:2 * h + 2], halves(f"xl{h}"), X))
                tsc(neg_max[:, 2 * h:2 * h + 2], neg_max[:, 2 * h:2 * h + 2], -256 ** -0.5, None, ALU.mult)\
                    .then_inc(signal("xmax"), 1)

            def cross_norm(h):
                ve.wait_ge(*read(f"xl{h}"))
                step(nc.vector.reciprocal(p_inv[:, 2 * h:2 * h + 2], p_sum[:, 2 * h:2 * h + 2]))
                for t in range(TT):
                    v = prob[:, h % 3, 256 * t:256 * t + 256]
                    ins = tsc(v, v, p_inv[:, 2 * h + t:2 * h + t + 1], None, ALU.mult)
                ins.then_inc(signal("xprob"), 1)

            def cross_gate(h):
                ve.wait_ge(*full(f"xo{h}"))
                stt(pair(zx, h), bank_of(f"xo{h}")[:, :], 0.5, pair(zx, h), ALU.mult, ALU.mult).then_inc(reader(f"xo{h}"), 1)

            top_keys(0)
            top_keys(1)
            step(tsc(pen, score, 0.5 * TAKEN, NEG, ALU.is_gt, ALU.mult))
            tt_(pen, pen, diag3, ALU.add).then_inc(signal("pen_ready"), 1)
            for j in range(4):
                twice_silu(f"zx{j}", pair(zx, j))
            cross_max(0)
            cross_max(1)
            cross_norm(0)
            cross_max(2)
            cross_norm(1)
            cross_max(3)
            cross_gate(0)
            cross_norm(2)
            for j in range(2):
                ve.wait_ge(*full(f"ax{j}"))
                ve.wait_ge(signal("gate_abs"), j + 1)
                for hh in range(2):
                    h = 2 * j + hh
                    ins = tsc(cumlog[:, h, :], bank_of(f"ax{j}")[:, 256 * hh:256 * hh + 256], b_gla[:, h:h + 1], 0.0,
                              ALU.add, ALU.min)
                ins.then_inc(reader(f"ax{j}"), 1)
            ve.wait_ge(*read("ax1"))
            ve.wait_ge(signal("gate_ln"), 1)
            step(tt_(cumlog, cumlog, expo, ALU.subtract))
            for h in range(H1):
                ins = nc.vector.tensor_tensor_scan(expo[:, h, :], const("keep"), cumlog[:, h, :], 0.0, ALU.mult, ALU.add)
            ins.then_inc(signal("gate_cum"), 1)
            cross_gate(1)
            cross_norm(3)
            cross_gate(2)
            cross_gate(3)
            ve.wait_ge(*read("gk1"))
            ve.wait_ge(signal("gate_cum"), 1)
            last = expo.rearrange("p h (c t) -> p (h c) t", t=CH)[:, :, CH - 1:CH].broadcast_to([128, 16, CH])
            tt_(expo_last.rearrange("p (a t) -> p a t", t=CH), last, expo.rearrange("p h (c t) -> p (h c) t", t=CH),
                ALU.subtract).then_inc(signal("gate_diff"), 1)
            ve.wait_ge(signal("gate_exp"), 2)
            stt(gq, gq, DK ** -0.5, cumlog, ALU.mult, ALU.mult)
            tt_(k_d, k_d, gk, ALU.mult).then_inc(signal("gla_kd"), 1)
            ve.wait_ge(signal("gate_exp"), 3)
            tt_(gk.rearrange("p a b -> p (a b)"), gk.rearrange("p a b -> p (a b)"), expo_last, ALU.mult)\
                .then_inc(signal("gla_kt"), 1)
            ve.wait_ge(signal("att_zero"), 1)
            for j in range(TT):
                ve.wait_ge(*full(f"at{j}"))
                m = const("chunk").bitcast(U32).unsqueeze(1).broadcast_to([128, 4, 128])
                nc.vector.copy_predicated(attT[:, 4 * j:4 * j + 4, :], m,
                                          bank_of(f"at{j}")[:, :].rearrange("p (h t) -> p h t", h=4))\
                    .then_inc(reader(f"at{j}"), 1)
            twice_silu("zg0", pair(zg, 0))
            twice_silu("zg1", pair(zg, 1))
            for c in range(NCH - 1):
                for j in range(2):
                    ve.wait_ge(*full(f"kv{c}{j}"))
                    for hh in range(2):
                        h = 2 * j + hh
                        s = slice(256 * h, 256 * h + 256)
                        src = bank_of(f"kv{c}{j}")[:, 256 * hh:256 * hh + 256]
                        if c == 0:
                            ins = nc.vector.tensor_copy(state[0][:, s], src)
                        else:
                            ins = stt(state[c][:, s], state[c - 1][:, s], decay1[:, 4 * h + c:4 * h + c + 1], src,
                                      ALU.mult, ALU.add)
                    ins.then_inc(reader(f"kv{c}{j}"), 1)
                    ve.wait_ge(*read(f"kv{c}{j}"))
            twice_silu("zg2", pair(zg, 2))
            twice_silu("zg3", pair(zg, 3))
            for h in range(H1):
                ve.wait_ge(*full(f"og{h}"))
                ve.wait_ge(signal("rstd_g"), h + 1)
                for t in range(TT):
                    ins = tsc(g_out[:, t, 256 * h:256 * h + 256], bank_of(f"og{h}")[:, 256 * t:256 * t + 256],
                              rstd[:, 8 + 2 * h + t:9 + 2 * h + t], None, ALU.mult)
                ins.then_inc(reader(f"og{h}"), 1)
            for j in range(4):
                twice_silu(f"zd{j}", pair(zd, j))
            for h in range(H1):
                ve.wait_ge(*full(f"yt{h}"))
                for c in range(2):
                    ins = stt(zg[:, 2 * h + c, :], bank_of(f"yt{h}")[:, 256 * c:256 * c + 256], g_gla_half[:, c:c + 1],
                              zg[:, 2 * h + c, :], ALU.mult, ALU.mult)
                ins.then_inc(reader(f"yt{h}"), 1)

            def causal_scores(pre, i, scale, add):
                name = f"{pre}l{i}"
                ve.wait_ge(*full(name))
                if i >= 3:
                    ve.wait_ge(*full(f"{pre}p{i - 3}"))
                p = prob[:, i % 3, 0:384]
                stt(p, bank_of(name)[:, 0:384], scale, add, ALU.mult, ALU.add).then_inc(reader(name), 1)
                ve.wait_ge(*read(name))
                c = 2 * (i % 8)
                nc.vector.reduce_max(neg_max[:, c:c + 1], p[:, 0:128], X, negate=True)
                nc.vector.reduce_max(neg_max[:, c + 1:c + 2], p[:, 128:384], X, negate=True).then_inc(signal(pre + "max"), 1)

            def causal_norm(pre, i, gate=None):
                ve.wait_ge(signal(pre + "exp"), i + 1)
                c = 2 * (i % 8)
                step(nc.vector.reciprocal(p_inv[:, c:c + 2], p_sum[:, c:c + 2]))
                if gate is not None:
                    step(tt_(p_inv[:, c:c + 2], p_inv[:, c:c + 2], gate, ALU.mult))
                for t, (a, b) in enumerate(((0, 128), (128, 384))):
                    v = prob[:, i % 3, a:b]
                    ins = tsc(v, v, p_inv[:, c + t:c + t + 1], None, ALU.mult)
                ins.then_inc(signal(pre + "prob"), 1)

            for h in range(DH + 2):
                if h < DH:
                    ve.wait_ge(signal("bias_pen"), h + 1)
                    causal_scores("d", h, 128 ** -0.5, bias_pen[:, h % 2, :])
                if 1 <= h <= DH:
                    causal_norm("d", h - 1)
                if h >= 3 and h % 2 == 1:
                    j = (h - 3) // 2
                    ve.wait_ge(*full(f"do{j}"))
                    stt(pair(zd, j), bank_of(f"do{j}")[:, :], 0.5, pair(zd, j), ALU.mult, ALU.mult)\
                        .then_inc(reader(f"do{j}"), 1)
            def low_part(n):
                name = split_units[n]
                m = 256 * ffn_tiles(name)
                ve.wait_ge(signal("w_high"), n + 1)
                tt_(w_lo[:, n % 2, 0:m], ring[:, order.index(name) % NSLOT, 0:m], w_hi[:, n % 2, 0:m].bitcast(F),
                    ALU.subtract).then_inc(signal("w_split"), 1)

            ve.wait_ge(signal("h1_high"), 1)
            tt_(h_lo[:, :, :], hT, h_hi[:, :, :].bitcast(F), ALU.subtract).then_inc(signal("h_split"), 1)
            low_part(0)
            low_part(1)
            for j in range(4):
                m = pair(merged, j)
                for b in range(3):
                    name = f"bo{b}{j}"
                    dst = m if b == 0 else relu[:, b - 1, :]
                    if 3 * j + b + 2 < nsg:
                        low_part(3 * j + b + 2)
                    ve.wait_ge(*read(f"sg{b}{j}"))
                    ve.wait_ge(*full(name))
                    stt(dst, tnh[:, tanh_users.index(name) % 2, :], 1.0, bank_of(name)[:, :], ALU.add, ALU.mult)\
                        .then_inc(reader(name), 1)
                    if b > 0:
                        ve.wait_ge(*read(name))
                        step(tt_(m, m, dst, ALU.add))
                tsc(m, m, 0.5, None, ALU.mult).then_inc(signal("merged1"), 1)
            ve.wait_ge(signal("rstd_wo"), 1)
            ve.wait_ge(signal("g_post_in"), 16)
            for t in range(TT):
                step(stt(xn[:, t, :], xn[:, t, :], rstd[:, 4 + t:5 + t], g_post, ALU.mult, ALU.mult))
            tt_(xres, xres, xn, ALU.add).then_inc(signal("x_mid"), 1)

            scale_rows("y", xn, xres, 0)
            transposed("y", hT)
            ve.wait_ge(*full("ba"))
            ve.wait_ge(signal("beta_tanh"), 1)
            tsc(row_beta, row_beta, 0.5, 0.5, ALU.mult, ALU.add)
            tsc(row_a, bank_of("ba")[0:4, 256:512], dt_bias, None, ALU.add).then_inc(reader("ba"), 1)
            ve.wait_ge(signal("alpha_ln"), 1)
            step(tsc(row_a, row_a, 0.0, None, ALU.max))
            step(tt_(row_a, row_a, row_b, ALU.add))
            step(tsc(row_g, row_a, a_pos, -1.0, ALU.mult, ALU.mult))
            nc.vector.tensor_tensor_scan(row_gc, const("keep")[0:4, :], row_g, 0.0, ALU.mult, ALU.add)\
                .then_inc(signal("row_gc"), 1)
            ve.wait_ge(signal("row_gc"), 1)
            rl = row_gc.rearrange("p (c t) -> p c t", t=CH)
            tt_(row_last.rearrange("p (c t) -> p c t", t=CH), rl[:, :, CH - 1:CH].broadcast_to([4, NCH, CH]), rl,
                ALU.subtract).then_inc(signal("row_diff"), 1)
            ve.wait_ge(*read("gates"))
            step(tsc(gate_tok, gate_tok, 0.5, 0.5, ALU.mult, ALU.add))
            ve.wait_ge(signal("row_exp"), 2)
            tt_(row_g, row_b, row_beta, ALU.mult).then_inc(signal("row_g"), 1)

            def silu_of(j):
                i = tanh_users.index(f"conv{j}")
                plain = [u for u in tanh_users[:i + 1] if not u.startswith("bo")]
                ve.wait_ge(signal("tanh_done"), len(plain))
                stt(pair(cv, j), tnh[:, i % 2, :], 1.0, pair(cv, j), ALU.add, ALU.mult).then_inc(signal("silu_done"), 1)

            ve.wait_ge(signal("conv_pad"), 1)
            for j in range(6):
                ve.wait_ge(*read(f"c{j}"))
                for tap in range(4):
                    for i in (2 * j, 2 * j + 1):
                        src, w = raw[:, i, tap:tap + S], conv_w[:, i, tap:tap + 1]
                        if tap == 0:
                            ins = tsc(cv[:, i, :], src, w, None, ALU.mult)
                        else:
                            ins = stt(cv[:, i, :], src, w, cv[:, i, :], ALU.mult, ALU.add)
                    if tap < 3:
                        step(ins)
                ins.then_inc(signal("conv_done"), 1)
                if j >= 1:
                    silu_of(j - 1)
            silu_of(5)
            for i, (name, a, n) in enumerate((("r0", 0, 2), ("r1", 2, 1), ("r2", 4, 2), ("r3", 6, 2))):
                ve.wait_ge(*full(name))
                sinb = const("sin").unsqueeze(1).broadcast_to([128, n, S])
                tmp = prob[:, i % 3, 0:n * S].rearrange("p (a b) -> p a b", a=n)
                tt_(tmp, bank_of(name)[:, 0:n * S].rearrange("p (a b) -> p a b", a=n), sinb, ALU.mult)\
                    .then_inc(reader(name), 1)
                ve.wait_ge(*read(name))
                ve.wait_ge(signal("rope_cos"), i + 1)
                tt_(ns[:, a:a + n, :], ns[:, a:a + n, :], tmp, ALU.add).then_inc(signal("rope_done"), 1)
            for j in range(2):
                twice_silu(f"z{j}", pair(z2, j))
            for kv in range(2):
                ve.wait_ge(*full(f"sh{kv}"))
                for g in range(2):
                    for q in range(2):
                        r = slice(64 * q, 64 * q + 64)
                        t_ = bank_of(f"sh{kv}")[r, 256 * g:256 * g + 256].rearrange("p (n s) -> p s n", s=16)
                        dst = cblk[kv][r, :, 15 * g:15 * g + 15]
                        for half in range(2):
                            ins = tt_(dst[:, 8 * half:8 * half + 8, :], t_[:, q::2, half:half + 15],
                                      cmp_pos[kv][r, 8 * half:8 * half + 8].unsqueeze(2).broadcast_to([64, 8, 15]), ALU.add)
                ins.then_inc(reader(f"sh{kv}"), 1)
            ve.wait_ge(*full("ss"))
            tsc(norm_cols, bank_of("ss")[:, 0:16], EPS, None, ALU.add).then_inc(reader("ss"), 1)
            ve.wait_ge(*read("cols"))
            ve.wait_ge(signal("egc"), 2)
            tsc(cols[:, :, 16:20], cols[:, :, 0:4], 0.5, None, ALU.mult)
            step(tsc(cols[:, :, 20:24], cols[:, :, 0:4], -1.0, None, ALU.mult))
            nc.vector.tensor_copy(decay1.rearrange("p (h c) -> p h c", h=4),
                                  egc.rearrange("p h (c t) -> p h c t", t=CH)[:, :, :, CH - 1]).then_inc(signal("decay2"), 1)
            for j in range(2):
                for t in range(TT):
                    src = halves(f"gb{j}")[:, :, 128 * t:128 * t + 128]
                    gc = cols[:, t, 12 + 2 * j:14 + 2 * j].unsqueeze(2).broadcast_to([128, 2, 128])
                    ins = tt_(nA[:, 4 * t + 2 * j:4 * t + 2 * j + 2, :], src, gc, ALU.subtract)
                ins.then_inc(reader(f"gb{j}"), 1)
            ve.wait_ge(*read("gb1"))
            step(tsc(qkT, nA, 0.0, None, ALU.min))
            tsc(nA, nA, 0.0, None, ALU.max).then_inc(signal("d_min"), 1)
            ve.wait_ge(*full("nr"))
            tsc(norm_rows, bank_of("nr")[0:8, 0:256], const("rowscale")[0:8, :], None, ALU.mult).then_inc(reader("nr"), 1)
            for j in range(4):
                ve.wait_ge(*full(f"rb{j}"))
                tt_(pair(cv, j), pair(cv, j), bank_of(f"rb{j}")[:, :], ALU.mult).then_inc(reader(f"rb{j}"), 1)
            ve.wait_ge(*full("hid"))
            ve.wait_ge(signal("hid_tanh"), 1)
            hb = bank_of("hid")[:, 0:64].rearrange("p (a b) -> p a b", a=2)[:, :, 0:30]
            stt(hid.rearrange("p (a b) -> p a b", a=2)[:, :, 0:30], pc[:, :, 0:30], 1.0, hb, ALU.add, ALU.mult)\
                .then_inc(reader("hid"), 1)

            def by_head(name):
                return bank_of(name)[:, :].rearrange("p (h c) -> p h c", h=4)

            def col4(t, a):
                return cols[:, t, a:a + 4].unsqueeze(2).broadcast_to([128, 4, 128])

            for t in range(TT):
                ve.wait_ge(*full(f"kk{t}"))
                s = slice(4 * t, 4 * t + 4)
                tt_(kbe[:, s, :], by_head(f"kk{t}"), col4(t, 4), ALU.mult)
                tt_(kdt[:, s, :], by_head(f"kk{t}"), col4(t, 8), ALU.mult).then_inc(reader(f"kk{t}"), 1)
            for t in range(TT):
                ve.wait_ge(*full(f"vt{t}"))
                tt_(vb[:, 4 * t:4 * t + 4, :], by_head(f"vt{t}"), col4(t, 16), ALU.mult).then_inc(reader(f"vt{t}"), 1)
            ve.wait_ge(signal("d_exp"), 2)
            for t in range(TT):
                ve.wait_ge(*full(f"kg{t}"))
                s = slice(4 * t, 4 * t + 4)
                tt_(nA[:, s, :], nA[:, s, :], by_head(f"kg{t}"), ALU.mult).then_inc(reader(f"kg{t}"), 1)
                ve.wait_ge(*read(f"kg{t}"))
                ins = tt_(nA[:, s, :], nA[:, s, :], col4(t, 20), ALU.mult)
            ins.then_inc(signal("nA_ready"), 1)
            for t in range(TT):
                ve.wait_ge(*full(f"qg{t}"))
                s = slice(4 * t, 4 * t + 4)
                tt_(qkT[:, s, :], qkT[:, s, :], by_head(f"qg{t}"), ALU.mult).then_inc(reader(f"qg{t}"), 1)
            for g in range(2):
                ve.wait_ge(*full(f"cs{g}"))
                for t in range(TT):
                    ph = pc[:, t, 64 * g:64 * g + 64].rearrange("p (h n) -> p h n", n=16)[:, :, 0:15]
                    bh = bank_of(f"cs{g}")[:, 64 * t:64 * t + 64].rearrange("p (h n) -> p h n", n=16)[:, :, 0:15]
                    cn = const("cneg")[:, 16 * t:16 * t + 15].unsqueeze(1).broadcast_to([128, 4, 15])
                    ins = stt(ph, bh, 64 ** -0.5, cn, ALU.mult, ALU.add)
                ins.then_inc(reader(f"cs{g}"), 1)
            ve.wait_ge(*read("cs1"))
            pcv = pc.rearrange("p t (h n) -> p (t h) n", n=16)[:, :, 0:15]

            def per_head(v):
                return v.unsqueeze(2).broadcast_to([128, 16, 15])

            step(nc.vector.reduce_max(neg_max, pcv, X))
            tt_(pcv, pcv, per_head(neg_max), ALU.subtract).then_inc(signal("cmax"), 1)
            ib = ident.unsqueeze(1).broadcast_to([128, 8, 128])
            ve.wait_ge(signal("level_mask"), 1)
            tt_(Tm, nAm[0], ib, ALU.add).then_inc(signal("T_start"), 1)
            for t in range(TT):
                ve.wait_ge(*full(f"t0{t}"))
                tt_(TmT[:, 4 * t:4 * t + 4, :], by_head(f"t0{t}"), ident.unsqueeze(1).broadcast_to([128, 4, 128]), ALU.add)\
                    .then_inc(reader(f"t0{t}"), 1)
            ve.wait_ge(signal("cexp"), 1)
            step(nc.vector.reduce_sum(p_sum, pcv, X))
            step(nc.vector.reciprocal(p_inv, p_sum))
            step(tt_(p_inv.rearrange("p (t h) -> p t h", t=TT), p_inv.rearrange("p (t h) -> p t h", t=TT),
                     gate_tok[:, :, 0:24:3], ALU.mult))
            step(tt_(pcv, pcv, per_head(p_inv), ALU.mult))
            for t in range(TT):
                ph = pc[:, t, :].rearrange("p (h n) -> p h n", n=16)[:, :, 0:15]
                cn = const("cvis")[:, 16 * t:16 * t + 15].unsqueeze(1).broadcast_to([128, 8, 15])
                ins = tt_(ph, ph, cn, ALU.mult)
            ins.then_inc(signal("cprob"), 1)

            def level_add(n):
                for t in range(TT):
                    s = slice(4 * t, 4 * t + 4)
                    ve.wait_ge(*full(f"xt{n}{t}"))
                    if n < 5:
                        tt_(Tm[:, s, :], Tm[:, s, :], by_head(f"xx{n}{t}"), ALU.add).then_inc(reader(f"xx{n}{t}"), 1)
                    tt_(TmT[:, s, :], TmT[:, s, :], by_head(f"xt{n}{t}"), ALU.add).then_inc(reader(f"xt{n}{t}"), 1)

            def nsa_scores(i):
                causal_scores("n", i, 64 ** -0.5, diag3)

            def nsa_norm(i):
                r, g, b = i // 4, (i // 2) % 2, i % 2
                causal_norm("n", i, gate_tok[:, :, 3 * (4 * g + r) + 1 + b])

            for n in range(1, 5):
                level_add(n)
            nsa_scores(0)
            nsa_scores(1)
            level_add(5)
            nsa_norm(0)

            def chunk_new(c):
                t, r = c // 2, slice(64 * (c % 2), 64 * (c % 2) + 64)
                s = slice(4 * t, 4 * t + 4)
                if c == 0:
                    ve.wait_ge(*read("u0"))
                    nc.vector.tensor_copy(v_new[r, s, :], u_tok[r, s, :]).then_inc(signal("v_new"), 1)
                else:
                    ve.wait_ge(*read(f"u{t}"))
                    ve.wait_ge(*full(f"ws{c}"))
                    tt_(v_new[r, s, :], u_tok[r, s, :], bank_of(f"ws{c}")[r, :].rearrange("p (h c) -> p h c", h=4),
                        ALU.subtract).then_inc(reader(f"ws{c}"), 1)

            def chunk_state(c):
                ve.wait_ge(*full(f"gs{c}"))
                for h in range(4):
                    s = slice(128 * h, 128 * h + 128)
                    src = bank_of(f"gs{c}")[:, s]
                    if c == 0:
                        ins = nc.vector.tensor_copy(gstate[0][:, s], src)
                    else:
                        ins = stt(gstate[c][:, s], gstate[c - 1][:, s], decay1[:, 4 * h + c:4 * h + c + 1], src,
                                  ALU.mult, ALU.add)
                ins.then_inc(reader(f"gs{c}"), 1)

            ve.wait_ge(signal("q_decayed"), 1)
            chunk_new(0)
            for i in range(16):
                if i + 2 < 16:
                    nsa_scores(i + 2)
                if i + 1 < 16:
                    nsa_norm(i + 1)
                if i in (0, 2, 4):
                    chunk_state(i // 2)
                if i in (1, 3, 5):
                    chunk_new((i + 1) // 2)
                if i == 6:
                    ve.wait_ge(signal("rstd_d"), 1)
                    for t in range(TT):
                        s = slice(4 * t, 4 * t + 4)
                        rb = rstd[:, 8 + 4 * t:12 + 4 * t].unsqueeze(2).broadcast_to([128, 4, 128])
                        tt_(nA[:, s, :], by_head(f"gd{t}"), rb, ALU.mult).then_inc(reader(f"gd{t}"), 1)
            for j in range(2):
                ve.wait_ge(*full(f"gt{j}"))
                stt(pair(z2, j), bank_of(f"gt{j}")[:, :], g_gdn_half, pair(z2, j), ALU.mult, ALU.mult)\
                    .then_inc(reader(f"gt{j}"), 1)
            for j in range(2):
                for half in range(2):
                    q = 2 * j + half
                    for name, g in ((f"bg{j}", ma), (f"bn{j}", mb)):
                        title = name + "ab"[half]
                        ve.wait_ge(*full(title))
                        stt(pair(g, q), pair(g, q), 1.0, bank_of(title)[:, :], ALU.add, ALU.mult).then_inc(reader(title), 1)
            for q in range(4):
                ve.wait_ge(*read(f"bn{q // 2}{'ab'[q % 2]}"))
                step(tt_(pair(ma, q), pair(ma, q), pair(mb, q), ALU.add))
                tsc(pair(ma, q), pair(ma, q), 0.5, None, ALU.mult).then_inc(signal("merged2"), 1)
            for j in range(4):
                ve.wait_ge(*full(f"w2o{j}"))
                v = xres[:, :, 256 * j:256 * j + 256]
                tt_(v, v, halves(f"w2o{j}"), ALU.add).then_inc(reader(f"w2o{j}"), 1)
            ve.wait_ge(*read("w2o3"))
            scale_rows("f", xn, xres, 4)
            for j in range(4):
                ve.wait_ge(*full(f"Tf{j}"))
                for kk in range(2):
                    k = 2 * j + kk
                    tsc(h_hi[:, k, :], bank_of(f"Tf{j}")[:, 256 * kk:256 * kk + 256], gain["f"][:, k:k + 1], None,
                        ALU.mult).then_inc(signal("h_high"), 1)
                ve.wait_ge(signal("h_high"), 2 * j + 2)
                for kk in range(2):
                    k = 2 * j + kk
                    ins = stt(h_lo[:, k, :], bank_of(f"Tf{j}")[:, 256 * kk:256 * kk + 256], gain["f"][:, k:k + 1],
                              h_hi[:, k, :].bitcast(F), ALU.mult, ALU.subtract)
                ins.then_inc(reader(f"Tf{j}"), 1)

            low_part(nsg)
            low_part(nsg + 1)
            for j in range(FT):
                name = f"gu{j}"
                low_part(nsg + j + 2)
                ve.wait_ge(*full(name))
                i = tanh_users.index(name)
                plain = [u for u in tanh_users[:i + 1] if not u.startswith("bo")]
                ve.wait_ge(signal("tanh_done"), len(plain))
                step(stt(prob[:, j % 2, 0:256], tnh[:, i % 2, 0:256], 1.0, bank_of(name)[:, 0:256], ALU.add, ALU.mult))
                f = prob[:, j % 2, 256:512]
                step(stt(f, prob[:, j % 2, 0:256], 0.5, bank_of(name)[:, 256:512], ALU.mult, ALU.mult))
                step(nc.vector.tensor_copy(f_hi[:, j, :], f))
                tt_(f_lo[:, j, :], f, f_hi[:, j, :].bitcast(F), ALU.subtract).then_inc(reader(name), 1)
            for n in range(FT + 2, len(ffn_units)):
                low_part(nsg + n)
            for c in range(4):
                ve.wait_ge(*full(f"wd{c}"))
                v = xres[:, :, 256 * c:256 * c + 256]
                tt_(v, v, halves(f"wd{c}"), ALU.add).then_inc(reader(f"wd{c}"), 1)
            ve.wait_ge(*read("wd3"))
            ve.wait_ge(signal("rstd_o"), 1)
            ve.wait_ge(signal("g_fin_in"), 16)
            for t in range(TT):
                ins = stt(xn[:, t, :], xres[:, t, :], rstd[:, 6 + t:7 + t], g_fin, ALU.mult, ALU.mult)
            ins.then_inc(signal("result"), 1)


def kernel(**inputs):
    import numpy as _np
    import concourse.bacc as _bacc
    from concourse import mybir as _mybir
    from concourse.bass_utils import run_bass_kernel_spmd as _run

    nc = _bacc.Bacc("TRN2", target_bir_lowering=False, num_devices=1)
    arrays, aps = {}, {}
    for name, value in list(inputs.items()) + [("shape_constants", shape_constants())]:
        a = _np.ascontiguousarray(value)
        arrays[f"in_{name}"] = a
        aps[name] = nc.dram_tensor(f"in_{name}", a.shape, _mybir.dt.from_np(a.dtype), kind="ExternalInput").ap()
    out = nc.dram_tensor("out_0", (1, S, D), _mybir.dt.float32, kind="ExternalOutput").ap()
    consts = aps.pop("shape_constants")
    build(nc, aps, consts, out)
    r = _run(nc, [arrays], core_ids=[0])
    return r.results[0]["out_0"]
```
